# Optimizing a Trainium2 kernel written in Bass

```python
import math
import jax, jax.numpy as jnp
from jax import lax
import numpy as np

D_MODEL = 1024
BATCH = 1
SEQ = 256
DEPTH = 2

CHUNK = 64
N_META = 16
SB_HEADS = 8
SB_HEAD_DIM = 64
SB_WIDTH = SB_HEADS * SB_HEAD_DIM
CONV_CH = D_MODEL // 2
CONV_K = 31
D_FF = 2816
Q_BLOCK = 128
NORM_EPS = 1e-6
LN_EPS = 1e-5
IN_SIZES = [SB_WIDTH, SB_WIDTH, SB_WIDTH, CONV_CH, CONV_CH, D_MODEL, D_MODEL]
IN_SPLITS = [int(s) for s in np.cumsum(IN_SIZES)[:-1]]
IN_WIDTH = int(sum(IN_SIZES))


def rmsnorm(x, g):
    xf = x.astype(jnp.float32)
    y = xf * lax.rsqrt(jnp.mean(xf * xf, axis=-1, keepdims=True) + NORM_EPS)
    return (y * g.astype(jnp.float32)).astype(x.dtype)

def layernorm(x, g, b):
    xf = x.astype(jnp.float32)
    mu = jnp.mean(xf, axis=-1, keepdims=True)
    var = jnp.mean(jnp.square(xf - mu), axis=-1, keepdims=True)
    y = (xf - mu) * lax.rsqrt(var + LN_EPS)
    return (y * g.astype(jnp.float32) + b.astype(jnp.float32)).astype(x.dtype)

def swiglu(x, w_gate, w_up, w_down):
    return (jax.nn.silu(x @ w_gate) * (x @ w_up)) @ w_down

def stick_breaking_attention(q, k, v):
    B, L, _ = q.shape
    Lp = ((L + Q_BLOCK - 1) // Q_BLOCK) * Q_BLOCK
    nb = Lp // Q_BLOCK

    def heads(a):
        a = a.reshape(B, L, SB_HEADS, SB_HEAD_DIM).transpose(0, 2, 1, 3).astype(jnp.float32)
        return jnp.pad(a, ((0, 0), (0, 0), (0, Lp - L), (0, 0)))

    qh, kh, vh = heads(q), heads(k), heads(v)
    scale = 1.0 / math.sqrt(SB_HEAD_DIM)
    q_blocks = qh.reshape(B, SB_HEADS, nb, Q_BLOCK, SB_HEAD_DIM).transpose(2, 0, 1, 3, 4)
    starts = jnp.arange(nb, dtype=jnp.int32) * Q_BLOCK
    key_pos = jnp.arange(Lp, dtype=jnp.int32)[None, :]

    def block(args):
        qb, start = args
        z = jnp.einsum('bhqd,bhkd->bhqk', qb, kh) * scale
        qpos = start + jnp.arange(Q_BLOCK, dtype=jnp.int32)[:, None]
        valid = key_pos < qpos
        log_keep = jnp.where(valid, jax.nn.log_sigmoid(-z), 0.0)
        after = lax.cumsum(log_keep, axis=3, reverse=True) - log_keep
        attn = jnp.where(valid, jnp.exp(jax.nn.log_sigmoid(z) + after), 0.0)
        return jnp.einsum('bhqk,bhkd->bhqd', attn, vh)

    out = lax.map(block, (q_blocks, starts))
    out = out.transpose(1, 2, 0, 3, 4).reshape(B, SB_HEADS, Lp, SB_HEAD_DIM)[:, :, :L]
    return out.transpose(0, 2, 1, 3).reshape(B, L, SB_WIDTH).astype(q.dtype)

def conformer_conv(a, b, conv_w, conv_b, ln_g, ln_b):
    u = a * jax.nn.sigmoid(b)
    y = lax.conv_general_dilated(
        u, conv_w[:, None, :].astype(u.dtype), window_strides=(1,),
        padding=[(CONV_K - 1, 0)],
        dimension_numbers=('NWC', 'WIO', 'NWC'), feature_group_count=CONV_CH)
    y = y + conv_b.astype(y.dtype)
    return jax.nn.silu(layernorm(y, ln_g, ln_b))

def hybrid_mixer(u, w_in, w_attn_out, conv_w, conv_b, conv_ln_g, conv_ln_b, w_conv_out, w_out):
    proj = u @ w_in
    q, k, v, a, b, g_sb, g_conv = jnp.split(proj, IN_SPLITS, axis=-1)
    y_sb = stick_breaking_attention(q, k, v) @ w_attn_out
    y_conv = conformer_conv(a, b, conv_w, conv_b, conv_ln_g, conv_ln_b) @ w_conv_out
    m = jax.nn.sigmoid(g_sb) * y_sb + jax.nn.sigmoid(g_conv) * y_conv
    return m @ w_out

def first_inputs(seed: int = 0) -> dict:
    key = jax.random.key(seed)
    ks = iter(jax.random.split(key, 32))

    def w(shape, fan_in, scale=1.0):
        return jax.random.normal(next(ks), shape, jnp.float32) * (scale * fan_in ** -0.5)

    def gain(shape):
        return 1.0 + 0.05 * jax.random.normal(next(ks), shape, jnp.float32)

    def bias(shape):
        return 0.02 * jax.random.normal(next(ks), shape, jnp.float32)

    L_ = DEPTH
    return {
        "x": jax.random.normal(next(ks), (BATCH, SEQ, D_MODEL), jnp.float32),
        "meta": jax.random.normal(next(ks), (N_META, D_MODEL), jnp.float32),
        "ffn1_norm": gain((L_, D_MODEL)),
        "ffn1_w_gate": w((L_, D_MODEL, D_FF), D_MODEL),
        "ffn1_w_up": w((L_, D_MODEL, D_FF), D_MODEL),
        "ffn1_w_down": w((L_, D_FF, D_MODEL), D_FF),
        "mix_norm": gain((L_, D_MODEL)),
        "w_in": w((L_, D_MODEL, IN_WIDTH), D_MODEL),
        "w_attn_out": w((L_, SB_WIDTH, D_MODEL), SB_WIDTH),
        "conv_w": w((L_, CONV_K, CONV_CH), CONV_K),
        "conv_b": bias((L_, CONV_CH)),
        "conv_ln_g": gain((L_, CONV_CH)),
        "conv_ln_b": bias((L_, CONV_CH)),
        "w_conv_out": w((L_, CONV_CH, D_MODEL), CONV_CH),
        "w_out": w((L_, D_MODEL, D_MODEL), D_MODEL),
        "ffn2_norm": gain((L_, D_MODEL)),
        "ffn2_w_gate": w((L_, D_MODEL, D_FF), D_MODEL),
        "ffn2_w_up": w((L_, D_MODEL, D_FF), D_MODEL),
        "ffn2_w_down": w((L_, D_FF, D_MODEL), D_FF),
        "final_norm": gain((D_MODEL,)),
    }

def first_block(x, meta, ffn1_norm, ffn1_w_gate, ffn1_w_up, ffn1_w_down, mix_norm, w_in,
              w_attn_out, conv_w, conv_b, conv_ln_g, conv_ln_b, w_conv_out, w_out,
              ffn2_norm, ffn2_w_gate, ffn2_w_up, ffn2_w_down, final_norm):
    B = x.shape[0]
    meta_b = jnp.broadcast_to(meta.astype(x.dtype)[None], (B, N_META, D_MODEL))
    h = jnp.concatenate([meta_b, x], axis=1)
    for l in range(DEPTH):
        h = h + 0.5 * swiglu(rmsnorm(h, ffn1_norm[l]), ffn1_w_gate[l], ffn1_w_up[l], ffn1_w_down[l])
        h = h + hybrid_mixer(rmsnorm(h, mix_norm[l]), w_in[l], w_attn_out[l], conv_w[l], conv_b[l],
                             conv_ln_g[l], conv_ln_b[l], w_conv_out[l], w_out[l])
        h = h + 0.5 * swiglu(rmsnorm(h, ffn2_norm[l]), ffn2_w_gate[l], ffn2_w_up[l], ffn2_w_down[l])
    h = rmsnorm(h, final_norm)
    return h[:, N_META:]


N_MIXERS = 4
RMS_EPS = 1e-6
D_FF_2 = ((8 * D_MODEL // 3 + 255) // 256) * 256
DA_HEAD_DIM = 64
DA_HEADS = D_MODEL // (2 * DA_HEAD_DIM)
DA_QBLOCK = 128
RT_HEADS = 4
RT_KEY_DIM = D_MODEL // RT_HEADS
RT_VAL_DIM = 2 * RT_KEY_DIM
RT_CHUNK = 128
SG_WIDTH = 3 * D_MODEL
SG_GROUPS = 8
SG_CHUNK = 128
LRU_WIDTH = ((4 * D_MODEL // 3 + 255) // 256) * 256
LRU_BLOCK = 128
LRU_BLOCKS = LRU_WIDTH // LRU_BLOCK
CONV_WIDTH = 4
RG_C = 8.0


def _rms(x, gain):
    x32 = x.astype(jnp.float32)
    y = x32 * lax.rsqrt(jnp.mean(x32 * x32, axis=-1, keepdims=True) + RMS_EPS)
    return (y * gain.astype(jnp.float32)).astype(x.dtype)

def _swiglu(xn, w_in, w_out):
    a, b = jnp.split(xn @ w_in, 2, axis=-1)
    return (jax.nn.silu(a) * b) @ w_out

def _lambda_init(layer_idx):
    return 0.8 - 0.6 * math.exp(-0.3 * layer_idx)

def _diff_attention(xn, w_in, q_gain, k_gain, lam, subln, w_out, lam_init):
    B, T, _ = xn.shape
    H, Dh = DA_HEADS, DA_HEAD_DIM
    q, k, v = jnp.split(xn @ w_in, 3, axis=-1)
    q = _rms(q.reshape(B, T, H, 2, Dh), q_gain) * (Dh ** -0.5)
    k = _rms(k.reshape(B, T, H, 2, Dh), k_gain)
    q = q.transpose(0, 2, 3, 1, 4)
    k = k.transpose(0, 2, 3, 1, 4)
    v = v.reshape(B, T, H, 2 * Dh).transpose(0, 2, 1, 3)
    lam32 = lam.astype(jnp.float32)
    lmbda = (jnp.exp(jnp.sum(lam32[0] * lam32[1])) - jnp.exp(jnp.sum(lam32[2] * lam32[3]))
             + lam_init)
    slopes = 2.0 ** (-8.0 * jnp.arange(1, H + 1, dtype=jnp.float32) / H)
    nb = T // DA_QBLOCK
    q_blocks = q.reshape(B, H, 2, nb, DA_QBLOCK, Dh).transpose(3, 0, 1, 2, 4, 5)
    key_pos = jnp.arange(T)

    def block(args):
        qb, n = args
        q_pos = n * DA_QBLOCK + jnp.arange(DA_QBLOCK)
        s = jnp.einsum('bhmqd,bhmkd->bhmqk', qb, k, preferred_element_type=jnp.float32)
        dist = (q_pos[:, None] - key_pos[None, :]).astype(jnp.float32)
        bias = jnp.where(dist >= 0, -slopes[:, None, None] * dist, -jnp.inf)
        p = jax.nn.softmax(s + bias[None, :, None], axis=-1)
        a = p[:, :, 0] - lmbda * p[:, :, 1]
        return jnp.einsum('bhqk,bhkd->bhqd', a.astype(v.dtype), v)

    o = lax.map(block, (q_blocks, jnp.arange(nb)))
    o = o.transpose(1, 0, 3, 2, 4).reshape(B, T, H, 2 * Dh)
    o = _rms(o, subln) * (1.0 - lam_init)
    return o.reshape(B, T, H * 2 * Dh).astype(xn.dtype) @ w_out

def _retention(xn, w_in, subln, w_out):
    B, T, _ = xn.shape
    H, Dk, Dv, C = RT_HEADS, RT_KEY_DIM, RT_VAL_DIM, RT_CHUNK
    nc = T // C
    proj = xn @ w_in
    q, k, v, g = jnp.split(proj, [H * Dk, 2 * H * Dk, 2 * H * Dk + H * Dv], axis=-1)

    def to_chunks(t, d):
        t = t.astype(jnp.float32).reshape(B, T, H, d).transpose(0, 2, 1, 3)
        return t.reshape(B, H, nc, C, d).transpose(2, 0, 1, 3, 4)

    qc = to_chunks(q, Dk)
    kc = to_chunks(k, Dk) * (Dk ** -0.5)
    vc = to_chunks(v, Dv)
    gamma = 1.0 - 2.0 ** (-5.0 - jnp.arange(H, dtype=jnp.float32))
    log_g = jnp.log(gamma)
    idx = jnp.arange(C, dtype=jnp.float32)
    diff = idx[:, None] - idx[None, :]
    decay_intra = jnp.where(diff >= 0, jnp.exp(jnp.maximum(diff, 0.0) * log_g[:, None, None]), 0.0)
    xi = jnp.exp((idx + 1.0) * log_g[:, None])
    zeta = jnp.exp((C - 1.0 - idx) * log_g[:, None])
    g_chunk = jnp.exp(C * log_g)

    def step(R, inp):
        qq, kk, vv = inp
        att = jnp.einsum('bhqd,bhkd->bhqk', qq, kk) * decay_intra
        o = (jnp.einsum('bhqk,bhkv->bhqv', att, vv)
             + jnp.einsum('bhqd,bhdv->bhqv', qq, R) * xi[:, :, None])
        R = g_chunk[:, None, None] * R + jnp.einsum('bhkd,bhkv->bhdv', kk * zeta[:, :, None], vv)
        return R, o

    R0 = jnp.zeros((B, H, Dk, Dv), jnp.float32)
    _, o = lax.scan(step, R0, (qc, kc, vc))
    o = o.transpose(1, 0, 3, 2, 4).reshape(B, T, H, Dv)
    o = _rms(o, subln).reshape(B, T, H * Dv)
    return (jax.nn.silu(g.astype(jnp.float32)) * o).astype(xn.dtype) @ w_out

def _spatial_gating(xn, w_in, v_gain, w_s, b_s, w_out):
    B, T, _ = xn.shape
    C, G = SG_CHUNK, SG_GROUPS
    nc = T // C
    z = jax.nn.gelu(xn @ w_in)
    u, v = jnp.split(z, 2, axis=-1)
    v = _rms(v, v_gain).reshape(B, nc, C, G, SG_WIDTH // G)
    ws = w_s * jnp.tril(jnp.ones((C, C), w_s.dtype))
    mixed = jnp.einsum('gts,bnsgc->bntgc', ws, v) + jnp.transpose(b_s)[None, None, :, :, None]
    return (u * mixed.reshape(B, T, SG_WIDTH)) @ w_out

def _rglru_block(xn, w_in, conv_w, conv_b, w_a, b_a, w_x, b_x, lam, w_out):
    B, T, _ = xn.shape
    gate_br, xb = jnp.split(xn @ w_in, 2, axis=-1)
    gate = jax.nn.gelu(gate_br)
    xb = lax.conv_general_dilated(
        xb, conv_w[:, None, :].astype(xb.dtype), window_strides=(1,),
        padding=[(CONV_WIDTH - 1, 0)], dimension_numbers=('NWC', 'WIO', 'NWC'),
        feature_group_count=LRU_WIDTH) + conv_b
    xb = xb.astype(jnp.float32)
    xblk = xb.reshape(B, T, LRU_BLOCKS, LRU_BLOCK)
    r = jax.nn.sigmoid(jnp.einsum('btnc,ncd->btnd', xblk, w_a.astype(jnp.float32))
                       .reshape(B, T, LRU_WIDTH) + b_a)
    i = jax.nn.sigmoid(jnp.einsum('btnc,ncd->btnd', xblk, w_x.astype(jnp.float32))
                       .reshape(B, T, LRU_WIDTH) + b_x)
    log_a = -RG_C * r * jax.nn.softplus(-lam.astype(jnp.float32))
    a = jnp.exp(log_a)
    b = jnp.sqrt(jnp.maximum(-jnp.expm1(2.0 * log_a), 1e-12)) * (i * xb)

    def combine(c1, c2):
        a1, b1 = c1
        a2, b2 = c2
        return a1 * a2, a2 * b1 + b2

    _, h = lax.associative_scan(combine, (a, b), axis=1)
    return (h * gate.astype(jnp.float32)).astype(xn.dtype) @ w_out

def second_inputs(seed: int = 0) -> dict:
    key = jax.random.key(seed)
    keys = iter(jax.random.split(key, 40))
    f32 = jnp.float32

    def nrm(shape, scale):
        return scale * jax.random.normal(next(keys), shape, f32)

    def gain(shape):
        return 1.0 + 0.02 * jax.random.normal(next(keys), shape, f32)

    na, nr, ns, nl = [len(range(m, DEPTH, N_MIXERS)) for m in range(N_MIXERS)]
    D = D_MODEL
    da_width = DA_HEADS * 2 * DA_HEAD_DIM
    rt_in = 2 * RT_HEADS * RT_KEY_DIM + 2 * RT_HEADS * RT_VAL_DIM
    inp = {}
    inp['x'] = jax.random.normal(next(keys), (BATCH, SEQ, D), f32)
    inp['ffn1_norm'] = gain((DEPTH, D))
    inp['ffn1_w_in'] = nrm((DEPTH, D, 2 * D_FF_2), D ** -0.5)
    inp['ffn1_w_out'] = nrm((DEPTH, D_FF_2, D), D_FF_2 ** -0.5)
    inp['mix_norm'] = gain((DEPTH, D))
    inp['ffn2_norm'] = gain((DEPTH, D))
    inp['ffn2_w_in'] = nrm((DEPTH, D, 2 * D_FF_2), D ** -0.5)
    inp['ffn2_w_out'] = nrm((DEPTH, D_FF_2, D), D_FF_2 ** -0.5)
    inp['da_w_in'] = nrm((na, D, 3 * da_width), D ** -0.5)
    inp['da_q_gain'] = gain((na, DA_HEAD_DIM))
    inp['da_k_gain'] = gain((na, DA_HEAD_DIM))
    inp['da_lambda'] = nrm((na, 4, DA_HEAD_DIM), 0.1)
    inp['da_subln'] = gain((na, 2 * DA_HEAD_DIM))
    inp['da_w_out'] = nrm((na, da_width, D), da_width ** -0.5)
    inp['rt_w_in'] = nrm((nr, D, rt_in), D ** -0.5)
    inp['rt_subln'] = gain((nr, RT_HEADS, RT_VAL_DIM))
    inp['rt_w_out'] = nrm((nr, RT_HEADS * RT_VAL_DIM, D), (RT_HEADS * RT_VAL_DIM) ** -0.5)
    inp['sg_w_in'] = nrm((ns, D, 2 * SG_WIDTH), D ** -0.5)
    inp['sg_v_gain'] = gain((ns, SG_WIDTH))
    inp['sg_w_s'] = nrm((ns, SG_GROUPS, SG_CHUNK, SG_CHUNK), SG_CHUNK ** -0.5)
    inp['sg_b_s'] = 1.0 + nrm((ns, SG_GROUPS, SG_CHUNK), 0.1)
    inp['sg_w_out'] = nrm((ns, SG_WIDTH, D), SG_WIDTH ** -0.5)
    inp['lr_w_in'] = nrm((nl, D, 2 * LRU_WIDTH), D ** -0.5)
    inp['lr_conv_w'] = nrm((nl, CONV_WIDTH, LRU_WIDTH), CONV_WIDTH ** -0.5)
    inp['lr_conv_b'] = nrm((nl, LRU_WIDTH), 0.01)
    inp['lr_w_a'] = nrm((nl, LRU_BLOCKS, LRU_BLOCK, LRU_BLOCK), LRU_BLOCK ** -0.5)
    inp['lr_b_a'] = nrm((nl, LRU_WIDTH), 0.01)
    inp['lr_w_x'] = nrm((nl, LRU_BLOCKS, LRU_BLOCK, LRU_BLOCK), LRU_BLOCK ** -0.5)
    inp['lr_b_x'] = nrm((nl, LRU_WIDTH), 0.01)
    a0 = jax.random.uniform(next(keys), (nl, LRU_WIDTH), f32, 0.9, 0.999)
    s = a0 ** (1.0 / RG_C)
    inp['lr_lambda'] = jnp.log(s) - jnp.log1p(-s)
    inp['lr_w_out'] = nrm((nl, LRU_WIDTH, D), LRU_WIDTH ** -0.5)
    return inp

def second_block(x, ffn1_norm, ffn1_w_in, ffn1_w_out, mix_norm, ffn2_norm, ffn2_w_in, ffn2_w_out,
              da_w_in, da_q_gain, da_k_gain, da_lambda, da_subln, da_w_out,
              rt_w_in, rt_subln, rt_w_out,
              sg_w_in, sg_v_gain, sg_w_s, sg_b_s, sg_w_out,
              lr_w_in, lr_conv_w, lr_conv_b, lr_w_a, lr_b_a, lr_w_x, lr_b_x, lr_lambda, lr_w_out):
    for i in range(DEPTH):
        kind = i % N_MIXERS
        j = i // N_MIXERS
        h = x + 0.5 * _swiglu(_rms(x, ffn1_norm[i]), ffn1_w_in[i], ffn1_w_out[i])
        xn = _rms(h, mix_norm[i])
        if kind == 0:
            m = _diff_attention(xn, da_w_in[j], da_q_gain[j], da_k_gain[j], da_lambda[j],
                                da_subln[j], da_w_out[j], _lambda_init(i))
        elif kind == 1:
            m = _retention(xn, rt_w_in[j], rt_subln[j], rt_w_out[j])
        elif kind == 2:
            m = _spatial_gating(xn, sg_w_in[j], sg_v_gain[j], sg_w_s[j], sg_b_s[j], sg_w_out[j])
        else:
            m = _rglru_block(xn, lr_w_in[j], lr_conv_w[j], lr_conv_b[j], lr_w_a[j], lr_b_a[j],
                             lr_w_x[j], lr_b_x[j], lr_lambda[j], lr_w_out[j])
        h = h + m.astype(h.dtype)
        x = h + 0.5 * _swiglu(_rms(h, ffn2_norm[i]), ffn2_w_in[i], ffn2_w_out[i])
    return x


def setup_inputs(seed=0):
    out = dict(first_inputs(seed))
    for name, value in second_inputs(seed + 1).items():
        if name != "x":
            out[name + "_2"] = value
    return out


def reference(
    x, meta, ffn1_norm, ffn1_w_gate, ffn1_w_up, ffn1_w_down, mix_norm, w_in, w_attn_out, conv_w,
    conv_b, conv_ln_g, conv_ln_b, w_conv_out, w_out, ffn2_norm, ffn2_w_gate, ffn2_w_up,
    ffn2_w_down, final_norm, ffn1_norm_2, ffn1_w_in_2, ffn1_w_out_2, mix_norm_2, ffn2_norm_2,
    ffn2_w_in_2, ffn2_w_out_2, da_w_in_2, da_q_gain_2, da_k_gain_2, da_lambda_2, da_subln_2,
    da_w_out_2, rt_w_in_2, rt_subln_2, rt_w_out_2, sg_w_in_2, sg_v_gain_2, sg_w_s_2, sg_b_s_2,
    sg_w_out_2, lr_w_in_2, lr_conv_w_2, lr_conv_b_2, lr_w_a_2, lr_b_a_2, lr_w_x_2, lr_b_x_2,
    lr_lambda_2, lr_w_out_2,
):
    x = first_block(
        x, meta, ffn1_norm, ffn1_w_gate, ffn1_w_up, ffn1_w_down, mix_norm, w_in, w_attn_out,
        conv_w, conv_b, conv_ln_g, conv_ln_b, w_conv_out, w_out, ffn2_norm, ffn2_w_gate,
        ffn2_w_up, ffn2_w_down, final_norm,
    )
    return second_block(
        x, ffn1_norm_2, ffn1_w_in_2, ffn1_w_out_2, mix_norm_2, ffn2_norm_2, ffn2_w_in_2,
        ffn2_w_out_2, da_w_in_2, da_q_gain_2, da_k_gain_2, da_lambda_2, da_subln_2, da_w_out_2,
        rt_w_in_2, rt_subln_2, rt_w_out_2, sg_w_in_2, sg_v_gain_2, sg_w_s_2, sg_b_s_2,
        sg_w_out_2, lr_w_in_2, lr_conv_w_2, lr_conv_b_2, lr_w_a_2, lr_b_a_2, lr_w_x_2, lr_b_x_2,
        lr_lambda_2, lr_w_out_2,
    )


_drawn_inputs = setup_inputs


def setup_inputs(seed=0):
    import zlib

    import numpy as np

    out = dict(_drawn_inputs(seed))
    spreads = {}
    factors = {'ffn1_norm_2': 3.791,
     'ffn2_norm_2': 5.923,
     'da_q_gain_2': 4.668,
     'da_k_gain_2': 5.247,
     'da_subln_2': 10.688,
     'rt_subln_2': 58.0}
    for name, (base, spread) in spreads.items():
        noise = np.random.default_rng([zlib.crc32(name.encode()), seed]).standard_normal(out[name].shape)
        drawn = base * np.exp(spread * noise) if base else spread * noise
        out[name] = __import__('jax').numpy.asarray(drawn.astype(out[name].dtype))
    for name, factor in factors.items():
        out[name] = (out[name] * factor).astype(out[name].dtype)
    return out
```

```python
import math
from contextlib import ExitStack

import numpy as np
import concourse.bass as bass
from concourse import mybir

D = 1024
KD = D // 128
META = 16
SEQ = 256
T = META + SEQ
FF = 2816
FT = FF // 128
HALF = FT // 2
K8 = KD * 128
K11 = HALF * 128
RING = 4
CONV_K = 31
CH = 4
SB_HEADS = 8
DA_HEADS = 8
RT_HEADS = 4
LAM_INIT = 0.8 - 0.6 * math.exp(0.0)
RMS_EPS = 1e-6
LN_EPS = 1e-5

PHASES = ["ffn", "mix", "ffn", "ffn", "mix", "ffn", "final", "ffn", "da", "ffn", "ffn", "rt", "ffn"]
FINAL = PHASES.index("final")
LAST_MIX = FINAL - 2
STREAM = {
    "ffn": [(2 * FT, K8), (2 * KD, K11)],
    "mix": [(36, K8), (8, K8), (8, K8)],
    "da": [(24, K8), (8, K8)],
    "rt": [(48, K8), (16, K8)],
    "final": [],
}
ACCS = {"ffn": 2 * FT, "mix": 36 + 16, "da": 24, "rt": 48, "final": 0}


def bases():
    out, p, p8, p11, a, f = [], 0, 0, 0, 0, 0
    for kind in PHASES:
        out.append(dict(P=p, P8=p8, P11=p11, A=a, F=f))
        for count, cols in STREAM[kind]:
            p += count
            if cols == K8:
                p8 += count
            else:
                p11 += count
        a += ACCS[kind]
        f += FT if kind == "ffn" else 0
    return out, p, p8, p11


BASE, PANELS, PANELS8, PANELS11 = bases()
COLS = [c for kind in PHASES for count, c in STREAM[kind] for _ in range(count)]


LN_EXP, SILU = "natural_log_exp_and_others", "silu_and_others"


def first_col(y):
    return 0 if y <= LAST_MIX else META


def u_base(y):
    return KD * (y if y <= FINAL else y - 1)


S_TILES = [(0, 0, T), (128, T, T - 128), (256, T + T - 128, T - 256)]
SW = S_TILES[2][1] + S_TILES[2][2]
PLACE = list(range(12, 20)) + list(range(4, 12)) + list(range(0, 4)) + list(range(20, 36))
A_SLOT, B_SLOT, V_SLOT, Q_SLOT, K_SLOT, G_SLOT = 12, 16, 0, 4, 8, 20
CPAD = CONV_K - 1
TAPS_AT = 5


def build(nc, w8, w11, xT, small, cst, lam, outT):
    f32 = mybir.dt.float32
    f32r = mybir.dt.float32r
    ALU = mybir.AluOpType
    ACT = mybir.ActivationFunctionType
    AX = mybir.AxisListType
    ctx = ExitStack()

    with ctx:
        def sb(name, shape, dt=f32, where=None):
            return (where or ctx).enter_context(nc.sbuf_tensor(name, shape, dt))

        def sem(name):
            return ctx.enter_context(nc.semaphore(name))

        raw = sb("raw", [128, RING, K11])
        whi = sb("whi", [128, RING, K11], f32r)
        wlo = sb("wlo", [128, RING, K11], f32r)
        h = sb("h", [128, KD, T])
        u_hi = sb("u_hi", [128, KD, T], f32r)
        u_lo = sb("u_lo", [128, KD, T], f32r)
        sq = sb("sq", [128, T])
        ssq = sb("ssq", [128, T])
        R = sb("R", [128, T])
        epsilons = sb("epsilons", [128, 3])
        rms_eps, ln_eps, one = (epsilons[:, i:i + 1] for i in range(3))
        consts = sb("consts", [128, 7, 128])
        mean_d, mean_512, mean_128, mean_64, ident, ones_f, tri_f = (consts[:, i, :] for i in range(7))
        ones_r = sb("ones_r", [128, 128], f32r)
        tri_r = sb("tri_r", [128, 128], f32r)
        gain = sb("gain", [128, len(PHASES), KD])
        sgain = sb("sgain", [128, 2 * CH * (CONV_K + 3) + 3 + 16])
        lam_in = sb("lam_in", [128, 4, 64])
        lam_p = sb("lam_p", [128, 2, 64])
        lam2 = sb("lam2", [128, 5])
        C0 = 2 * CH * (CONV_K + 3)

        def conv_w(l, c, k):
            return sgain[:, (l * CH + c) * (CONV_K + 3) + k:(l * CH + c) * (CONV_K + 3) + k + 1]

        q_raw, k_gain, sub_raw = (sgain[:, C0 + j:C0 + j + 1] for j in range(3))
        q_gain, sub_gain = lam2[:, 3:4], lam2[:, 4:5]

        def rt_gain(j):
            return sgain[:, C0 + 3 + j:C0 + 4 + j]

        with ExitStack() as area:
            hid_hi = sb("hid_hi", [128, FT, T], f32r, area)
            hid_lo = sb("hid_lo", [128, FT, T], f32r, area)
            gt = sb("gt", [128, 2, T], f32, area)
            up = sb("up", [128, 2, T], f32, area)
            sl = sb("sl", [128, 2, T], f32, area)
            pr = sb("pr", [128, 2, T], f32, area)
        with ExitStack() as area:
            proj = sb("proj", [128, 36, T], f32, area)
            cpad = sb("cpad", [128, CH, CPAD + T], f32, area)
            qk = sb("qk", [128, 16, T], f32r, area)
            v_hi = sb("v_hi", [128, 3, 512], f32r, area)
            v_lo = sb("v_lo", [128, 3, 512], f32r, area)
            ez = sb("ez", [128, SW], f32, area)
            nlk = sb("nlk", [128, SW], f32, area)
            ls = sb("ls", [128, 2, SW], f32, area)
            ex = sb("ex", [128, SW], f32, area)
            lk_hi = sb("lk_hi", [128, SW], f32r, area)
            lk_lo = sb("lk_lo", [128, SW], f32r, area)
            at_hi = sb("at_hi", [128, 2, SW], f32r, area)
            at_lo = sb("at_lo", [128, 2, SW], f32r, area)
            ao_hi = sb("ao_hi", [128, 4, T], f32r, area)
            ao_lo = sb("ao_lo", [128, 4, T], f32r, area)
            smask = sb("smask", [128, SW], f32, area)
        with ExitStack() as area:
            dist = sb("dist", [128, 384], f32, area)
            dqk = sb("dqk", [128, 2, 2, SEQ], f32, area)
            dsq = sb("dsq", [128, 2, SEQ], f32, area)
            drq = sb("drq", [128, 2, SEQ], f32, area)
            dn = sb("dn", [128, 2, SEQ], f32, area)
            dn_hi = sb("dn_hi", [128, 2, SEQ], f32r, area)
            dn_lo = sb("dn_lo", [128, 2, SEQ], f32r, area)
            dv = sb("dv", [128, SEQ], f32, area)
            dv_hi = sb("dv_hi", [128, 2, SEQ], f32r, area)
            dv_lo = sb("dv_lo", [128, 2, SEQ], f32r, area)
            dsc = sb("dsc", [128, 2, 384], f32, area)
            dp = sb("dp", [128, 2, 384], f32, area)
            dst = sb("dst", [128, 16], f32, area)
            dt1 = sb("dt1", [128, 384], f32, area)
            da_ = sb("da_", [128, 384], f32, area)
            dT_hi = sb("dT_hi", [128, 384], f32r, area)
            dT_lo = sb("dT_lo", [128, 384], f32r, area)
            do_ = sb("do_", [128, SEQ], f32, area)
            dosq = sb("dosq", [128, SEQ], f32, area)
            dro = sb("dro", [128, SEQ], f32, area)
            don = sb("don", [128, SEQ], f32, area)
            dy_hi = sb("dy_hi", [128, DA_HEADS, SEQ], f32r, area)
            dy_lo = sb("dy_lo", [128, DA_HEADS, SEQ], f32r, area)
        with ExitStack() as area:
            rdist = sb("rdist", [128, 384], f32, area)
            rqk = sb("rqk", [128, 2, 4, SEQ], f32, area)
            rqk_hi = sb("rqk_hi", [128, 2, 4, SEQ], f32r, area)
            rqk_lo = sb("rqk_lo", [128, 2, 4, SEQ], f32r, area)
            rv = sb("rv", [128, 4, SEQ], f32, area)
            rv_hi = sb("rv_hi", [128, 2, 512], f32r, area)
            rv_lo = sb("rv_lo", [128, 2, 512], f32r, area)
            rdec = sb("rdec", [128, 384], f32, area)
            rat = sb("rat", [128, 384], f32, area)
            rat_hi = sb("rat_hi", [128, 384], f32r, area)
            rat_lo = sb("rat_lo", [128, 384], f32r, area)
            ro = sb("ro", [128, 16, SEQ], f32, area)
            rosq = sb("rosq", [128, 4, SEQ], f32, area)
            rro = sb("rro", [128, SEQ], f32, area)
            rg = sb("rg", [128, 2, SEQ], f32, area)
            rsg = sb("rsg", [128, 2, SEQ], f32, area)
            rp = sb("rp", [128, 2, SEQ], f32, area)
            ry_hi = sb("ry_hi", [128, 16, SEQ], f32r, area)
            ry_lo = sb("ry_lo", [128, 16, SEQ], f32r, area)

        bank = [ctx.enter_context(nc.psum_tensor(f"bank{i}", [128, 512], f32)) for i in range(8)]
        NORM = bank[7]

        raw_loaded = [sem(f"raw_loaded{i}") for i in range(RING)]
        hi_ready, lo_ready, panel_used = sem("hi_ready"), sem("lo_ready"), sem("panel_used")
        a_evac = sem("a_evac")
        h_done, u_hi_ready, u_ready = sem("h_done"), sem("u_hi_ready"), sem("u_ready")
        sq_done, ssq_done = sem("sq_done"), sem("ssq_done")
        norm_full, log_done, R_ready, eps_set = (sem(s) for s in ("norm_full", "log_done", "R_ready", "eps_set"))
        silu_done, prod_done = sem("silu_done"), sem("prod_done")
        hid_hi_ready, hid_ready = sem("hid_hi_ready"), sem("hid_ready")
        gain_loaded, const_loaded, const_r = (sem(s) for s in ("gain_loaded", "const_loaded", "const_r"))
        x_loaded = [sem(f"x_loaded{i}") for i in range(2)]
        lam_step, lam_exp, table_loaded, stored = (sem(s) for s in ("lam_step", "lam_exp", "table_loaded", "stored"))
        pad_done, b_gate, cin_done, tap_done = (sem(s) for s in ("pad_done", "b_gate", "cin_done", "tap_done"))
        ysum_step, mu_full, yc_done, ysq_done = (sem(s) for s in ("ysum_step", "mu_full", "yc_done", "ysq_done"))
        var_full, r2_done, yn_done, ysilu = (sem(s) for s in ("var_full", "r2_done", "yn_done", "ysilu"))
        co_hi_ready, co_ready, m_done = (sem(s) for s in ("co_hi_ready", "co_ready", "m_done"))
        m_hi_ready, m_ready, gate_done = (sem(s) for s in ("m_hi_ready", "m_ready", "gate_done"))
        r2_log, d_ro_log, d_rq_log, r_ro_log = (
            sem(s) for s in ("r2_log", "d_ro_log", "d_rq_log", "r_ro_log"))
        qk_hi_ready, qk_ready, vt_full, v_hi_ready, v_ready = (
            sem(s) for s in ("qk_hi_ready", "qk_ready", "vt_full", "v_hi_ready", "v_ready"))
        z_full, az_done, e_done, l_done, nlk_done = (
            sem(s) for s in ("z_full", "az_done", "e_done", "l_done", "nlk_done"))
        ls_done, nlk_masked, lk_hi_ready, lk_ready, c_full = (
            sem(s) for s in ("ls_done", "nlk_masked", "lk_hi_ready", "lk_ready", "c_full"))
        arg_done, ex_done, ex_masked, at_hi_ready, at_ready = (
            sem(s) for s in ("arg_done", "ex_done", "ex_masked", "at_hi_ready", "at_ready"))
        o_full, ao_hi_ready, ao_ready = (sem(s) for s in ("o_full", "ao_hi_ready", "ao_ready"))
        d_sq_done, d_qksum, d_rq_done, d_n_done, d_n_hi, d_n_ready = (
            sem(s) for s in ("d_sq_done", "d_qksum", "d_rq_done", "d_n_done", "d_n_hi", "d_n_ready"))
        d_vt_full, d_v_hi, d_v_ready, d_s_full, d_sc_done, d_max_done = (
            sem(s) for s in ("d_vt_full", "d_v_hi", "d_v_ready", "d_s_full", "d_sc_done", "d_max_done"))
        d_nmax, d_exps, d_rec, d_c1, d_t1, d_a_done = (
            sem(s) for s in ("d_nmax", "d_exps", "d_rec", "d_c1", "d_t1", "d_a_done"))
        d_t_full, d_T_hi, d_T_ready, d_av_full, d_o_done, d_osq = (
            sem(s) for s in ("d_t_full", "d_T_hi", "d_T_ready", "d_av_full", "d_o_done", "d_osq"))
        d_osum, d_ro_done, d_on_done, d_y_hi, d_y_ready = (
            sem(s) for s in ("d_osum", "d_ro_done", "d_on_done", "d_y_hi", "d_y_ready"))
        r_vt_full, r_v_hi, r_v_ready, r_qk_hi, r_qk_ready, r_s_full = (
            sem(s) for s in ("r_vt_full", "r_v_hi", "r_v_ready", "r_qk_hi", "r_qk_ready", "r_s_full"))
        r_dec, r_at_done, r_at_hi, r_at_ready, r_av_full, r_o_done = (
            sem(s) for s in ("r_dec", "r_at_done", "r_at_hi", "r_at_ready", "r_av_full", "r_o_done"))
        r_osq, r_osum, r_ro_done, r_on_done = (sem(s) for s in ("r_osq", "r_osum", "r_ro_done", "r_on_done"))
        r_silu, r_p_done, r_y_hi, r_y_ready = (sem(s) for s in ("r_silu", "r_p_done", "r_y_hi", "r_y_ready"))

        block = ctx.enter_context(nc.Block())

        def win(y):
            return slice(first_col(y), T)

        def width(y):
            return T - first_col(y)


        def products(pe, out, slot, k, x_hi, x_lo, first, last):
            w_h, w_l = whi[:, slot, k * 128:k * 128 + 128], wlo[:, slot, k * 128:k * 128 + 128]
            pe.matmul(out, w_h, x_hi, start=first, stop=False)
            pe.matmul(out, w_h, x_lo, start=False, stop=False)
            return pe.matmul(out, w_l, x_hi, start=False, stop=last)

        def act_split(act, n, it=0):
            if not isinstance(it, int) or n < PANELS:
                act.wait_ge(raw_loaded[n % RING], 16 * (n // RING + 1) + 16 * it)
                if n >= RING:
                    act.wait_ge(panel_used, n - RING + 1 + RING * it)
                act.activation(whi[:, n % RING, 0:COLS[n]], raw[:, n % RING, 0:COLS[n]],
                               ACT.Copy).then_inc(hi_ready, 1)

        def dve_split(dve, n, it=0):
            if not isinstance(it, int) or n < PANELS:
                dve.wait_ge(hi_ready, n + 1 + RING * it)
                dve.tensor_tensor(wlo[:, n % RING, 0:COLS[n]], raw[:, n % RING, 0:COLS[n]],
                                  whi[:, n % RING, 0:COLS[n]], ALU.subtract).then_inc(lo_ready, 1)

        def act_update(act, y, f):
            if y == FINAL or y == len(PHASES):
                return
            act.wait_ge(h_done, KD * y + f + 1)
            act.activation(u_hi[:, f, win(y)], h[:, f, win(y)], ACT.Copy,
                           scale=gain[:, y, f:f + 1]).then_inc(u_hi_ready, 1)

        def dve_update(dve, y, f):
            if y == FINAL or y == len(PHASES):
                return
            dve.wait_ge(u_hi_ready, u_base(y) + f + 1)
            dve.scalar_tensor_tensor(out=u_lo[:, f, win(y)], in0=h[:, f, win(y)],
                                     scalar=gain[:, y, f:f + 1], in1=u_hi[:, f, win(y)],
                                     op0=ALU.mult, op1=ALU.subtract).then_inc(u_ready, 1)

        def pool_update(pool, y):
            for f in range(KD):
                pool.wait_ge(h_done, KD * y + f + 1)
                if f == 0:
                    if y > 0:
                        pool.wait_ge(norm_full, y)
                    pool.tensor_tensor(ssq[:, win(y)], h[:, f, win(y)], h[:, f, win(y)],
                                       ALU.mult).then_inc(ssq_done, 1)
                else:
                    pool.wait_ge(ssq_done, KD * y + f)
                    pool.tensor_tensor(sq[:, win(y)], h[:, f, win(y)], h[:, f, win(y)],
                                       ALU.mult).then_inc(sq_done, 1)
                    pool.wait_ge(sq_done, (KD - 1) * y + f)
                    pool.tensor_tensor(ssq[:, win(y)], ssq[:, win(y)], sq[:, win(y)],
                                       ALU.add).then_inc(ssq_done, 1)

        def norm_step(t):
            return 0 if t <= RT_HEADS else 1

        def pe_norm(pe, y):
            if y == 0:
                pe.wait_ge(gain_loaded, 32)
            pe.wait_ge(ssq_done, KD * (y + 1))
            pe.matmul(NORM[:, 0:width(y)], mean_d, ssq[:, win(y)],
                      start=True, stop=True).then_inc(norm_full, 1)

        def act_norm(act, y):
            act.preload_act_table_set(LN_EXP)
            act.wait_ge(norm_full, y + 1)
            act_rsqrt(act, R[:, win(y)], NORM[:, 0:width(y)], rms_eps, log_done, y + 1, R_ready)

        def act_rsqrt(act, out, src, eps, log_done, count, done):
            act.activation(out, src, ACT.Ln, bias=eps).then_inc(log_done, 1)
            act.wait_ge(log_done, count)
            act.activation(out, out, ACT.Exp, scale=-0.5).then_inc(done, 1)


        @block.sync
        def _(sp):
            def load_x(i):
                half = KD // 2
                sp.dma_start(proj[:, half * i:half * i + half, :],
                             xT[D // 2 * i:D // 2 * (i + 1), :].rearrange("(f p) t -> p f t", p=128))\
                  .then_inc(x_loaded[i], 16)

            load_x(0)

            def panels(n0, count, src, d0, cols):
                def group(it, empty=False):
                    for j in range(RING):
                        n = n0 + j
                        if not empty:
                            sp.wait_ge(lo_ready, n - RING + 1 + RING * it)
                        sp.dma_start(raw[:, n % RING, 0:cols], src[d0 + j + RING * it, :, :])\
                          .then_inc(raw_loaded[n % RING], 16)
                        if empty and j == 0:
                            load_x(1)
                first = 1 if n0 == 0 else 0
                if first:
                    group(0, empty=True)
                with sp.Fori(first, count // RING) as it:
                    group(it)

            for y, kind in enumerate(PHASES):
                b = BASE[y]
                n, d8 = b["P"], b["P8"]
                for count, cols in STREAM[kind]:
                    if cols == K8:
                        panels(n, count, w8, d8, cols)
                        d8 += count
                    else:
                        panels(n, count, w11, b["P11"], cols)
                    n += count
            for f in range(KD):
                sp.wait_ge(h_done, KD * len(PHASES) + f + 1)
                sp.dma_start(outT[f * 128:f * 128 + 128, :], h[:, f, META:T]).then_inc(stored, 16)
            sp.wait_ge(stored, 16 * KD)


        @block.tensor
        def _(pe):
            def ffn(y):
                b, N, W = BASE[y], width(y), win(y)

                def gate_up(it, norm=False):
                    for j in range(RING):
                        n, g = b["P"] + j, b["A"] + j
                        pe.wait_ge(lo_ready, n + 1 + RING * it)
                        if g + RING * it >= RING if isinstance(it, int) else True:
                            pe.wait_ge(a_evac, g - 3 + RING * it)
                        for k in range(KD):
                            if norm and j == 0 and y == 0:
                                pe.wait_ge(u_ready, k + 1)
                            elif norm and j == 0 and k in (0, KD - 2, KD - 1):
                                pe.wait_ge(u_ready, u_base(y) + (KD - 2 if k == 0 else k + 1))
                            mm = products(pe, bank[g % 4][:, 0:N], n % RING, k, u_hi[:, k, W],
                                          u_lo[:, k, W], k == 0, k == KD - 1)
                        mm.then_inc(panel_used, 1)
                        if norm and j == 0:
                            pe_norm(pe, y)

                gate_up(0, norm=True)
                with pe.Fori(1, 2 * FT // RING) as it:
                    gate_up(it)
                out_proj(y, b["P"] + 2 * FT, 2, HALF, lambda k: (hid_hi[:, k, W], hid_lo[:, k, W]),
                         hid_ready, b["F"] + FT, N)

            def out_proj(y, n0, per_tile, tiles, x, ready, count, N):
                group = RING // per_tile
                with pe.Fori(0, KD // group) as it:
                    for j in range(group):
                        pe.wait_ge(h_done, KD * (y + 1) + j - 1 + group * it)
                        for q in range(per_tile):
                            n = n0 + per_tile * j + q
                            pe.wait_ge(lo_ready, n + 1 + RING * it)
                            for k in range(tiles):
                                K, last = q * tiles + k, per_tile * tiles - 1
                                if j == 0 and K in (0, last - 1, last):
                                    pe.wait_ge(ready, count - (2 if K == 0 else last - K))
                                mm = products(pe, bank[4 + j % 2][:, 0:N], n % RING, k, *x(K),
                                              K == 0, K == last)
                            mm.then_inc(panel_used, 1)

            def mix(y, l):
                b = BASE[y]
                P, A = b["P"], b["A"]
                W2, N2 = win(y + 1), width(y + 1)
                flat = qk[:, :, :].rearrange("p a t -> p (a t)")

                def in_panel(j, it=0, cols=T):
                    pe.wait_ge(lo_ready, P + j + 1 + RING * it)
                    pe.wait_ge(a_evac, A + j - 3 + RING * it)
                    for k in range(KD):
                        if j == 0 and isinstance(it, int) and k in (0, KD - 2, KD - 1):
                            pe.wait_ge(u_ready, u_base(y) + (KD - 2 if k == 0 else k + 1))
                        mm = products(pe, bank[(A + j) % 4][:, 0:cols], (P + j) % RING, k, u_hi[:, k, T - cols:T],
                                      u_lo[:, k, T - cols:T], k == 0, k == KD - 1)
                    mm.then_inc(panel_used, 1)

                def scores(hd):
                    if hd == 0:
                        pe.wait_ge(qk_ready, 8 * (l + 1))
                    if SB_HEADS * l + hd > 0:
                        pe.wait_ge(ls_done, SB_HEADS * l + hd)
                    rows, f = slice(64 * (hd % 2), 64 * (hd % 2) + 64), hd // 2
                    for i, (s0, c0, w) in enumerate(S_TILES):
                        for n, (kt, qt) in enumerate(((0, 8), (0, 12), (4, 8))):
                            ks, qs = (kt + f) * T + s0, (qt + f) * T + s0
                            mm = pe.matmul(bank[6][:, c0:c0 + w], flat[rows, ks:ks + 128],
                                           flat[rows, qs:qs + w], start=(i == 0 and n == 0),
                                           stop=(n == 2), skip_group_check=True)
                    mm.then_inc(z_full, 1)

                def transpose_v():
                    pe.wait_ge(a_evac, A + 20)
                    vf = proj[:, :, :].rearrange("p a t -> p (a t)")
                    for i, (bk, (s0, _, _)) in enumerate(zip((4, 5, 7), S_TILES)):
                        for f in range(4):
                            at = (V_SLOT + f) * T + s0
                            mm = pe.transpose(bank[bk][:, f * 128:f * 128 + 128], vf[:, at:at + 128], ident)
                        mm.then_inc(vt_full, 1)

                def suffix_sums(hd):
                    pe.wait_ge(lk_ready, SB_HEADS * l + hd + 1)
                    if hd == 0:
                        pe.wait_ge(v_ready, 3 * (l + 1))
                    else:
                        pe.wait_ge(arg_done, SB_HEADS * l + hd)
                    for n, lk in enumerate((lk_hi, lk_lo)):
                        for i, (s0, c0, w) in enumerate(S_TILES):
                            for i2, (s2, c2, w2) in enumerate(S_TILES[i:]):
                                at = c0 + s2 - s0
                                mm = pe.matmul(bank[4][:, at:at + w2], (ones_r if i2 else tri_r)[:, :],
                                               lk[:, c2:c2 + w2], start=(n == 0 and i == 0 and i2 == 0),
                                               stop=(n == 1), skip_group_check=True)
                    mm.then_inc(c_full, 1)

                def weighted_values(hd):
                    pe.wait_ge(at_ready, SB_HEADS * l + hd + 1)
                    if hd == 0:
                        pe.wait_ge(v_ready, 3 * (l + 1))
                    else:
                        pe.wait_ge(ao_ready, SB_HEADS * l + hd)
                    cols = slice(128 * (hd // 2), 128 * (hd // 2) + 128)
                    for i, (s0, c0, w) in enumerate(S_TILES):
                        for n, (vv, at) in enumerate(((v_hi, at_hi), (v_hi, at_lo), (v_lo, at_hi))):
                            mm = pe.matmul(bank[5][:, s0:T], vv[:, i, cols], at[:, hd % 2, c0:c0 + w],
                                           start=(i == 0 and n == 0), stop=(i == 2 and n == 2),
                                           skip_group_check=True)
                    mm.then_inc(o_full, 1)

                pe.wait_ge(const_r, 2)
                in_panel(0)
                pe_norm(pe, y)
                for j in range(1, 4):
                    in_panel(j)
                with pe.Fori(1, 5) as it:
                    for j in range(RING):
                        in_panel(j, it)
                for t in range(SB_HEADS + 2):
                    if t < SB_HEADS:
                        scores(t)
                        in_panel(20 + 2 * t, cols=N2)
                    if t == 0:
                        transpose_v()
                    if 1 <= t <= SB_HEADS:
                        suffix_sums(t - 1)
                    if t < SB_HEADS:
                        in_panel(21 + 2 * t, cols=N2)
                    if t >= 2:
                        weighted_values(t - 2)

                pe.wait_ge(ysum_step, 3 * (l + 1))
                pe.matmul(bank[7][:, 0:N2], mean_512, sq[:, W2], start=True, stop=True).then_inc(mu_full, 1)
                for part in range(2):
                    x_hi, x_lo = ((ao_hi, ao_lo), (u_hi, u_lo))[part]
                    for p in range(4):
                        n = P + 36 + 4 * part + p
                        pe.wait_ge(lo_ready, n + 1)
                        if p == 0:
                            if part == 0:
                                pe.wait_ge(ao_ready, SB_HEADS * (l + 1))
                            else:
                                pe.wait_ge(co_ready, CH * (l + 1))
                        for ff in range(2):
                            g = A + 36 + 8 * part + 2 * p + ff
                            pe.wait_ge(a_evac, g - 3)
                            for k in range(4):
                                mm = products(pe, bank[g % 4][:, 0:N2], n % RING, 4 * ff + k, x_hi[:, k, W2],
                                              x_lo[:, k, W2], k == 0, k == 3)
                        mm.then_inc(panel_used, 1)
                        if part == 0 and p == 1:
                            pe.wait_ge(ysq_done, CH * (l + 1))
                            for c in range(CH):
                                mm = pe.matmul(bank[6][:, 0:N2], mean_512, cpad[:, c, CPAD:CPAD + N2],
                                               start=(c == 0), stop=(c == CH - 1))
                            mm.then_inc(var_full, 1)
                out_proj(y, P + 44, 1, KD, lambda k: (qk[:, k, W2], qk[:, KD + k, W2]), m_ready,
                         KD * (l + 1), N2)

            def in_panel2(y, j):
                b = BASE[y]
                pe.wait_ge(lo_ready, b["P"] + j + 1)
                pe.wait_ge(a_evac, b["A"] + j - 1)
                for k in range(KD):
                    if j == 0 and k in (0, KD - 2, KD - 1):
                        pe.wait_ge(u_ready, u_base(y) + (KD - 2 if k == 0 else k + 1))
                    mm = products(pe, bank[j % 2][:, 0:SEQ], (b["P"] + j) % RING, k, u_hi[:, k, META:T],
                                  u_lo[:, k, META:T], k == 0, k == KD - 1)
                mm.then_inc(panel_used, 1)

            def da(y):
                b = BASE[y]

                def out_tiles(f0, f1, k0, k1):
                    if k0 == 0:
                        pe.wait_ge(a_evac, b["A"] + 24)
                    pe.wait_ge(d_y_ready, k1)
                    for f in range(f0, f1):
                        n = b["P"] + 24 + f
                        if k0 == 0:
                            pe.wait_ge(lo_ready, n + 1)
                        for k in range(k0, k1):
                            first = f % 2 == 0 and k == 0
                            w_h, w_l = (w[:, n % RING, k * 128:k * 128 + 128] for w in (whi, wlo))
                            for i, (w, x) in enumerate(((w_h, dy_hi), (w_h, dy_lo), (w_l, dy_hi))):
                                mm = pe.matmul(bank[f // 2][:, SEQ * (f % 2):SEQ * (f % 2) + SEQ], w, x[:, k, :],
                                               start=(first and i == 0), stop=(k == KD - 1 and i == 2),
                                               skip_group_check=True)
                        if k1 == KD:
                            mm.then_inc(panel_used, 1)

                for t in range(DA_HEADS + 3):
                    if t < DA_HEADS:
                        in_panel2(y, 3 * t)
                    if t == 0:
                        pe_norm(pe, y)
                    if t >= 3:
                        hd = t - 3
                        pe.wait_ge(d_T_ready, hd + 1)
                        if hd >= 1:
                            pe.wait_ge(d_o_done, hd)
                        for i, (c0, t0) in enumerate(((0, 0), (256, 128))):
                            for n, (vv, aa) in enumerate(((dv_hi, dT_hi), (dv_hi, dT_lo), (dv_lo, dT_hi))):
                                mm = pe.matmul(bank[3][:, t0:SEQ], vv[:, hd % 2, 128 * i:128 * i + 128],
                                               aa[:, c0:c0 + SEQ - t0], start=(i == 0 and n == 0),
                                               stop=(i == 1 and n == 2), skip_group_check=True)
                        mm.then_inc(d_av_full, 1)
                    if 1 <= t <= DA_HEADS:
                        pe.wait_ge(a_evac, b["A"] + 3 * t)
                        for i in range(2):
                            mm = pe.transpose(bank[2][:, 128 * i:128 * i + 128],
                                              dv[:, 128 * i:128 * i + 128], ident)
                        mm.then_inc(d_vt_full, 1)
                        pe.wait_ge(d_sq_done, 2 * t)
                        pe.matmul(bank[4][:, :], mean_64, dsq[:, :, :].rearrange("p a t -> p (a t)"),
                                  start=True, stop=True).then_inc(d_qksum, 1)
                    if t < DA_HEADS:
                        in_panel2(y, 3 * t + 1)
                    elif t == DA_HEADS:
                        out_tiles(0, 2, 0, 5)
                    else:
                        out_tiles(0, RING, t - 4, t - 3)
                    if t >= 3:
                        pe.wait_ge(d_osq, t - 2)
                        pe.matmul(bank[5][:, 0:SEQ], mean_128, dosq[:, :], start=True,
                                  stop=True).then_inc(d_osum, 1)
                    if t < DA_HEADS:
                        in_panel2(y, 3 * t + 2)
                    elif t == DA_HEADS:
                        out_tiles(2, RING, 0, 5)
                    if 2 <= t <= DA_HEADS + 1:
                        pe.wait_ge(d_a_done, 2 * (t - 1))
                        pe.wait_ge(d_v_ready, min(t, DA_HEADS))
                        for dst, src in ((0, 0), (128, 128), (256, 256)):
                            mm = pe.transpose(bank[2][:, dst:dst + 128], da_[:, src:src + 128], ident)
                        mm.then_inc(d_t_full, 1)
                    if 1 <= t <= DA_HEADS:
                        hd = t - 1
                        pe.wait_ge(d_n_ready, hd + 1)
                        if hd >= 1:
                            pe.wait_ge(d_sc_done, 2 * hd)
                        for m in range(2):
                            rows = slice(64 * m, 64 * m + 64)
                            for i, (c0, w) in enumerate(((0, 128), (128, 256))):
                                for n, (qq, kk) in enumerate(((dn_hi, dn_hi), (dn_hi, dn_lo), (dn_lo, dn_hi))):
                                    mm = pe.matmul(bank[6 + m][:, c0:c0 + w],
                                                   qq[rows, 0, 128 * i:128 * i + 128], kk[rows, 1, 0:w],
                                                   start=(i == 0 and n == 0), stop=(n == 2),
                                                   skip_group_check=True)
                        mm.then_inc(d_s_full, 1)
                out_tiles(0, RING, DA_HEADS - 1, DA_HEADS)
                for f in range(RING, KD):
                    n = b["P"] + 24 + f
                    pe.wait_ge(lo_ready, n + 1)
                    if f >= RING + 2:
                        pe.wait_ge(h_done, KD * (y + 1) + f - 1)
                    for k in range(KD):
                        mm = products(pe, bank[4 + f % 2][:, 0:SEQ], n % RING, k, dy_hi[:, k, :], dy_lo[:, k, :],
                                      k == 0, k == KD - 1)
                    mm.then_inc(panel_used, 1)

            def rt(y):
                b = BASE[y]
                for t in range(RT_HEADS + 2):
                    for c in range(8):
                        in_panel2(y, 8 * t + c)
                        if t == 0 and c == 0:
                            pe_norm(pe, y)
                        if not 1 <= t <= RT_HEADS:
                            continue
                        hd = t - 1
                        if c == 0:
                            pe.wait_ge(a_evac, b["A"] + 8 * t)
                            if hd >= 1:
                                pe.wait_ge(r_v_ready, 2 * hd)
                            for i in range(2):
                                for f in range(4):
                                    mm = pe.transpose(bank[2 + i][:, f * 128:f * 128 + 128],
                                                      rv[:, f, 128 * i:128 * i + 128], ident)
                                mm.then_inc(r_vt_full, 1)
                            pe.wait_ge(r_qk_ready, hd + 1)
                            if hd >= 1:
                                pe.wait_ge(r_at_done, hd)
                            p = hd % 2
                            for i, (s0, c0, w) in enumerate(((0, 0, 256), (128, 256, 128))):
                                for f in range(2):
                                    for n, (kk, qq) in enumerate(((rqk_hi, rqk_hi), (rqk_hi, rqk_lo), (rqk_lo, rqk_hi))):
                                        mm = pe.matmul(bank[6][:, c0:c0 + w], kk[:, p, 2 + f, s0:s0 + 128],
                                                       qq[:, p, f, s0:SEQ],
                                                       start=(i == 0 and f == 0 and n == 0),
                                                       stop=(f == 1 and n == 2), skip_group_check=True)
                            mm.then_inc(r_s_full, 1)
                        if c == 4:
                            pe.wait_ge(r_at_ready, hd + 1)
                            pe.wait_ge(r_v_ready, 2 * (hd + 1))
                            if hd >= 1:
                                pe.wait_ge(r_o_done, 2 * hd)
                            for f in range(4):
                                for i, (c0, t0) in enumerate(((0, 0), (256, 128))):
                                    for n, (vv, aa) in enumerate(((rv_hi, rat_hi), (rv_hi, rat_lo), (rv_lo, rat_hi))):
                                        at = 256 * (f % 2) + t0
                                        mm = pe.matmul(bank[4 + f // 2][:, at:at + SEQ - t0],
                                                       vv[:, i, f * 128:f * 128 + 128], aa[:, c0:c0 + SEQ - t0],
                                                       start=(f % 2 == 0 and i == 0 and n == 0),
                                                       stop=(i == 1 and n == 2), skip_group_check=True)
                            mm.then_inc(r_av_full, 1)
                        if c == 7:
                            pe.wait_ge(r_osq, hd + 1)
                            if hd >= 1:
                                pe.wait_ge(r_ro_done, hd)
                            for f in range(4):
                                mm = pe.matmul(bank[7][:, 0:SEQ], mean_512, rosq[:, f, :], start=(f == 0),
                                               stop=(f == 3))
                            mm.then_inc(r_osum, 1)
                out_proj(y, b["P"] + 48, 2, KD, lambda k: (ry_hi[:, k, :], ry_lo[:, k, :]), r_y_ready,
                         16, SEQ)

            layer = 0
            for y, kind in enumerate(PHASES):
                if kind == "ffn":
                    ffn(y)
                elif kind == "mix":
                    mix(y, layer)
                    layer += 1
                elif kind == "final":
                    pe_norm(pe, y)
                elif kind == "da":
                    da(y)
                else:
                    rt(y)


        @block.scalar
        def _(act):
            act.dma_start(gain[:, :, :], small[:, 0:GAINS].rearrange("p (y f) -> p y f", f=KD))\
               .then_inc(gain_loaded, 16)
            act.dma_start(mean_d, cst[:, 0:128]).then_inc(gain_loaded, 16)
            act.wait_ge(gain_loaded, 32)
            for f in range(KD // 2):
                act_update(act, 0, f)
            act_split(act, 0)
            for f in range(KD // 2, KD):
                act_update(act, 0, f)
            for n in range(1, RING):
                act_split(act, n)
            act.wait_ge(eps_set, 3)

            def out_proj(y, n0, per_tile):
                for f in range(KD):
                    if per_tile == 1 and f < KD - 1:
                        act_split(act, n0 + f + RING)
                        act_update(act, y + 1, f)
                        continue
                    act_update(act, y + 1, f)
                    for q in range(per_tile):
                        act_split(act, n0 + per_tile * f + q + RING)

            def ffn(y):
                b, W = BASE[y], win(y)

                act_norm(act, y)

                def pair(it):
                    for p in range(2):
                        f, g, F = 2 * it + p, b["A"] + 2 * p, b["F"] + p
                        act.wait_ge(a_evac, g + 1 + RING * it)
                        act.activation(sl[:, p, W], gt[:, p, W], ACT.Silu).then_inc(silu_done, 1)
                        act_split(act, b["P"] + 2 * p + RING, it)
                        act_split(act, b["P"] + 2 * p + 1 + RING, it)
                        act.wait_ge(prod_done, F + 1 + 2 * it)
                        act.activation(hid_hi[:, f, W], pr[:, p, W], ACT.Copy).then_inc(hid_hi_ready, 1)

                act.preload_act_table_set(SILU)
                with act.Fori(0, FT // 2 - 1) as it:
                    pair(it)
                for p in range(2):
                    f = FT - 2 + p
                    n = b["P"] + 2 * f
                    act.wait_ge(a_evac, b["A"] + 2 * f + 1)
                    act.activation(sl[:, p, W], gt[:, p, W], ACT.Silu).then_inc(silu_done, 1)
                    act_split(act, n + RING)
                    act_split(act, n + 1 + RING)
                    act.wait_ge(prod_done, b["F"] + f + 1)
                    act.activation(hid_hi[:, f, W], pr[:, p, W], ACT.Copy).then_inc(hid_hi_ready, 1)
                out_proj(y, b["P"] + 2 * FT, 2)

            def mix(y, l):
                b = BASE[y]
                P, A, H = b["P"], b["A"], SB_HEADS * l
                W2, N2 = win(y + 1), width(y + 1)
                act_norm(act, y)
                for j in range(20):
                    act_split(act, P + j + RING)
                    if 4 <= j < 8:
                        act.wait_ge(a_evac, A + j + 1)
                        act.activation(proj[:, B_SLOT + j - 4, :], proj[:, B_SLOT + j - 4, :],
                                       ACT.Sigmoid).then_inc(b_gate, 1)
                    if 8 <= j < 16:
                        i = j - 8
                        act.wait_ge(a_evac, A + j + 1)
                        act.activation(qk[:, 8 + i if i < 4 else i - 4, :], proj[:, PLACE[j], :],
                                       ACT.Copy).then_inc(qk_hi_ready, 1)
                act.preload_act_table_set(LN_EXP)
                for t in range(SB_HEADS + 3):
                    if t < SB_HEADS:
                        act.wait_ge(z_full, H + t + 1)
                        if t >= 1:
                            act.wait_ge(ls_done, H + t)
                        act.activation(ez[:, :], bank[6][:, 0:SW], ACT.Abs).then_inc(az_done, 1)
                        act.wait_ge(az_done, H + t + 1)
                        act.activation(ez[:, :], ez[:, :], ACT.Exp, scale=-1.0).then_inc(e_done, 1)
                        act.wait_ge(e_done, H + t + 1)
                        act.activation(ez[:, :], ez[:, :], ACT.Ln, bias=one).then_inc(l_done, 1)
                    if t >= 3:
                        hd = t - 3
                        rows = slice(64 * (hd % 2), 64 * (hd % 2) + 64)
                        act.wait_ge(o_full, H + hd + 1)
                        act.activation(ao_hi[rows, hd // 2, :], bank[5][rows, 0:T], ACT.Copy)\
                           .then_inc(ao_hi_ready, 1)
                    if t < SB_HEADS:
                        act_split(act, P + 20 + 2 * t + RING)
                    if t == 0:
                        for i, bk in enumerate((4, 5, 7)):
                            act.wait_ge(vt_full, 3 * l + i + 1)
                            act.activation(v_hi[:, i, :], bank[bk][:, :], ACT.Copy).then_inc(v_hi_ready, 1)
                    if t < SB_HEADS:
                        act.wait_ge(nlk_masked, H + t + 1)
                        if t >= 1:
                            act.wait_ge(c_full, H + t)
                        act.activation(lk_hi[:, :], nlk[:, :], ACT.Copy).then_inc(lk_hi_ready, 1)
                    if 1 <= t <= SB_HEADS:
                        act.wait_ge(arg_done, H + t)
                        act.activation(ex[:, :], ex[:, :], ACT.Exp).then_inc(ex_done, 1)
                    if t < SB_HEADS:
                        act_split(act, P + 21 + 2 * t + RING)
                    if 1 <= t <= SB_HEADS:
                        hd = t - 1
                        act.wait_ge(ex_masked, H + hd + 1)
                        if hd >= 2:
                            act.wait_ge(o_full, H + hd - 1)
                        act.activation(at_hi[:, hd % 2, :], ex[:, :], ACT.Copy).then_inc(at_hi_ready, 1)
                    if t in (4, 8):
                        eight = proj[:, G_SLOT + 2 * (t - 4):G_SLOT + 2 * t, W2]
                        act.wait_ge(a_evac, A + 20 + 2 * t)
                        act.activation(eight, eight, ACT.Sigmoid).then_inc(gate_done, 1)
                        act.preload_act_table_set(LN_EXP)
                for c in range(CH):
                    act.wait_ge(yc_done, CH * l + c + 1)
                    act.activation(cpad[:, c, CPAD:CPAD + N2], proj[:, A_SLOT + c, W2], ACT.Square)\
                       .then_inc(ysq_done, 1)
                act_split(act, P + 36 + RING)
                act_split(act, P + 37 + RING)
                act.wait_ge(var_full, l + 1)
                act_rsqrt(act, sq[:, W2], bank[6][:, 0:N2], ln_eps, r2_log, l + 1, r2_done)
                for c in range(CH):
                    act.wait_ge(yn_done, CH * l + c + 1)
                    act.activation(proj[:, A_SLOT + c, W2], proj[:, A_SLOT + c, W2], ACT.Silu,
                                   scale=conv_w(l, c, CONV_K + 1), bias=conv_w(l, c, CONV_K + 2))\
                       .then_inc(ysilu, 1)
                    act.wait_ge(ysilu, CH * l + c + 1)
                    if c == 0:
                        act.wait_ge(panel_used, P + 36)
                    act.activation(u_hi[:, c, W2], proj[:, A_SLOT + c, W2], ACT.Copy).then_inc(co_hi_ready, 1)
                act_split(act, P + 38 + RING)
                act_split(act, P + 39 + RING)
                for p in range(4):
                    act_split(act, P + 40 + p + RING)
                    for f in (2 * p, 2 * p + 1):
                        act.wait_ge(m_done, KD * l + f + 1)
                        act.activation(qk[:, f, W2], proj[:, G_SLOT + f, W2], ACT.Copy).then_inc(m_hi_ready, 1)
                out_proj(y, P + 44, 1)

            def da(y):
                b = BASE[y]
                P, A = b["P"], b["A"]
                act_norm(act, y)
                for t in range(DA_HEADS + 3):
                    if 2 <= t <= DA_HEADS + 1:
                        act.wait_ge(d_nmax, t - 1)
                        for i, (c0, w) in enumerate(((0, 128), (128, 256))):
                            for m in range(2):
                                j = 2 * i + m
                                act.activation(dp[:, m, c0:c0 + w], dsc[:, m, c0:c0 + w], ACT.Exp,
                                               bias=dst[:, 4 + j:5 + j], accum_out=dst[:, 8 + j:9 + j])\
                                   .then_inc(d_exps, 1)
                    if t < DA_HEADS:
                        act_split(act, P + 3 * t + RING)
                    if 1 <= t <= DA_HEADS:
                        act.wait_ge(d_vt_full, t)
                        act.activation(dv_hi[:, (t - 1) % 2, :], bank[2][:, 0:SEQ], ACT.Copy).then_inc(d_v_hi, 1)
                        act.wait_ge(d_qksum, t)
                        act_rsqrt(act, drq[:, :, :].rearrange("p a t -> p (a t)"), bank[4][:, :], rms_eps,
                                  d_rq_log, t, d_rq_done)
                    if t >= 3:
                        act.wait_ge(d_o_done, t - 2)
                        act.activation(dosq[:, :], do_[:, :], ACT.Square).then_inc(d_osq, 1)
                    if 1 <= t <= DA_HEADS:
                        act.wait_ge(d_n_done, 2 * t)
                        act.activation(dn_hi[:, :, :], dn[:, :, :], ACT.Copy).then_inc(d_n_hi, 1)
                    if t < DA_HEADS:
                        act_split(act, P + 3 * t + 1 + RING)
                    if t >= 3:
                        act.wait_ge(d_osum, t - 2)
                        act_rsqrt(act, dro[:, :], bank[5][:, 0:SEQ], rms_eps, d_ro_log, t - 2, d_ro_done)
                    if t < DA_HEADS:
                        act_split(act, P + 3 * t + 2 + RING)
                        act.wait_ge(a_evac, A + 3 * t + 2)
                        for i in range(2):
                            act.activation(dsq[:, i, :], dqk[:, t % 2, i, :], ACT.Square).then_inc(d_sq_done, 1)
                    if t >= 3:
                        act.wait_ge(d_on_done, t - 2)
                        act.activation(dy_hi[:, t - 3, :], don[:, :], ACT.Copy).then_inc(d_y_hi, 1)
                    if 2 <= t <= DA_HEADS + 1:
                        act.wait_ge(d_t_full, t - 1)
                        act.activation(dT_hi[:, :], bank[2][:, 0:384], ACT.Copy).then_inc(d_T_hi, 1)
                out_proj(y, P + 24, 1)

            def rt(y):
                b = BASE[y]
                P, A = b["P"], b["A"]
                act_norm(act, y)

                def gated_hi(j):
                    act.wait_ge(r_p_done, j + 1)
                    act.activation(ry_hi[:, j, :], rp[:, j % 2, :], ACT.Copy).then_inc(r_y_hi, 1)

                for t in range(RT_HEADS + 2):
                    for c in range(8):
                        j = 8 * (t - RT_HEADS) + c
                        if 2 <= t and c == norm_step(t):
                            act.wait_ge(r_osum, t - 1)
                            act_rsqrt(act, rro[:, :], bank[7][:, 0:SEQ], rms_eps, r_ro_log, t - 1, r_ro_done)
                        if 1 <= t <= RT_HEADS and c == 0:
                            hd = t - 1
                            if hd == 0:
                                act.wait_ge(table_loaded, 16 * 4)
                            else:
                                act.wait_ge(r_at_done, hd)
                            act.activation(rdec[:, :], rdist[:, :], ACT.Exp,
                                           scale=math.log(1.0 - 2.0 ** (-5 - hd))).then_inc(r_dec, 1)
                        if t >= RT_HEADS:
                            act.wait_ge(a_evac, A + 8 * t + c + 1)
                            act.activation(rsg[:, c % 2, :], rg[:, c % 2, :], ACT.Silu).then_inc(r_silu, 1)
                        act_split(act, P + 8 * t + c + RING)
                        if j >= 1:
                            gated_hi(j - 1)
                        if t < RT_HEADS and c == 3:
                            act.wait_ge(a_evac, A + 8 * t + 4)
                            act.activation(rqk_hi[:, t % 2, :, :], rqk[:, t % 2, :, :], ACT.Copy).then_inc(r_qk_hi, 1)
                        if not 1 <= t <= RT_HEADS:
                            continue
                        hd = t - 1
                        if c == 0:
                            for i in range(2):
                                act.wait_ge(r_vt_full, 2 * hd + i + 1)
                                act.activation(rv_hi[:, i, :], bank[2 + i][:, :], ACT.Copy).then_inc(r_v_hi, 1)
                        if c == 2:
                            act.wait_ge(r_at_done, hd + 1)
                            act.activation(rat_hi[:, :], rat[:, :], ACT.Copy).then_inc(r_at_hi, 1)
                        if c == 5:
                            act.wait_ge(r_o_done, 2 * (hd + 1))
                            act.activation(rosq[:, :, :], ro[:, 4 * hd:4 * hd + 4, :], ACT.Square).then_inc(r_osq, 1)
                gated_hi(15)
                out_proj(y, P + 48, 2)

            layer = 0
            for y, kind in enumerate(PHASES):
                if kind == "ffn":
                    ffn(y)
                elif kind == "mix":
                    mix(y, layer)
                    layer += 1
                elif kind == "final":
                    act_norm(act, y)
                    act.wait_ge(lam_step, 2)
                    act.activation(lam2[:, 0:2], lam2[:, 0:2], ACT.Exp).then_inc(lam_exp, 1)
                    for f in range(KD):
                        act_update(act, y + 1, f)
                elif kind == "da":
                    da(y)
                else:
                    rt(y)


        @block.vector
        def _(dve):
            for tile, value in ((rms_eps, RMS_EPS), (ln_eps, LN_EPS), (one, 1.0)):
                dve.memset(tile, value).then_inc(eps_set, 1)
            dve.wait_ge(gain_loaded, 32)
            half = KD // 2
            for i in range(2):
                dve.wait_ge(x_loaded[i], 16)
                for f in range(half * i, half * i + half):
                    dve.tensor_copy(h[:, f, :], proj[:, f, :]).then_inc(h_done, 1)
                for f in range(half * i, half * i + half):
                    dve_update(dve, 0, f)
                if i == 0:
                    dve_split(dve, 0)
            for n in range(1, RING):
                dve_split(dve, n)
            dve.wait_ge(const_loaded, CONST_LOADS * 16)
            dve.tensor_copy(ones_r[:, :], ones_f).then_inc(const_r, 1)
            dve.tensor_copy(tri_r[:, :], tri_f).then_inc(const_r, 1)

            def out_proj(y, n0, per_tile, factor, N, sources=None):
                W = win(y if N == width(y) else y + 1)
                for f in range(KD):
                    src = sources[f] if sources else bank[4 + f % 2][:, 0:N]
                    dve.wait_ge(panel_used, n0 + (f // 2 * 2 + 2 if sources and f < RING else per_tile * (f + 1)))
                    dve.scalar_tensor_tensor(out=h[:, f, W], in0=src, scalar=factor,
                                             in1=h[:, f, W], op0=ALU.mult, op1=ALU.add).then_inc(h_done, 1)
                    if per_tile == 1 and f > 0:
                        dve_update(dve, y + 1, f - 1)
                    if f == KD - 1:
                        dve_update(dve, y + 1, f)
                    for q in range(per_tile):
                        dve_split(dve, n0 + per_tile * f + q + RING)
                        if per_tile == 2 and q == 0 and f < KD - 1:
                            dve_update(dve, y + 1, f)

            def ffn(y):
                b, N, W = BASE[y], width(y), win(y)

                def tile(n, g, F, f, p, it, last):
                    it4, it2 = (RING * it, 2 * it) if not last else (0, 0)
                    dve.wait_ge(panel_used, n + 1 + it4)
                    dve.tensor_tensor(gt[:, p, W], bank[g % 4][:, 0:N], R[:, W], ALU.mult).then_inc(a_evac, 1)
                    dve.wait_ge(panel_used, n + 2 + it4)
                    dve.tensor_tensor(up[:, p, W], bank[(g + 1) % 4][:, 0:N], R[:, W], ALU.mult).then_inc(a_evac, 1)
                    dve_split(dve, n + RING, it)
                    dve.wait_ge(silu_done, F + 1 + it2)
                    dve.wait_ge(a_evac, g + 2 + it4)
                    dve.tensor_tensor(pr[:, p, W], sl[:, p, W], up[:, p, W], ALU.mult).then_inc(prod_done, 1)
                    dve_split(dve, n + 1 + RING, it)
                    dve.wait_ge(hid_hi_ready, F + 1 + it2)
                    dve.tensor_tensor(hid_lo[:, f, W], pr[:, p, W], hid_hi[:, f, W], ALU.subtract)\
                       .then_inc(hid_ready, 1)

                dve.wait_ge(R_ready, y + 1)
                with dve.Fori(0, FT // 2 - 1) as it:
                    for p in range(2):
                        tile(b["P"] + 2 * p, b["A"] + 2 * p, b["F"] + p, 2 * it + p, p, it, False)
                for p in range(2):
                    f = FT - 2 + p
                    tile(b["P"] + 2 * f, b["A"] + 2 * f, b["F"] + f, f, p, 0, True)
                out_proj(y, b["P"] + 2 * FT, 2, 0.5, N)

            def mix(y, l):
                b = BASE[y]
                P, A, H = b["P"], b["A"], SB_HEADS * l
                W2, N2 = win(y + 1), width(y + 1)
                f0 = T - N2
                cacc = proj[:, A_SLOT:A_SLOT + CH, :]
                taps = CH * CONV_K
                state = {"tap": 0}

                def read_out(j):
                    dve.wait_ge(panel_used, P + j + 1)
                    cols = T if j < 20 else N2
                    src, dst = bank[(A + j) % 4][:, 0:cols], proj[:, PLACE[j], T - cols:T]
                    if 8 <= j < 12:
                        dve.scalar_tensor_tensor(out=dst, in0=src, scalar=64 ** -0.5, in1=R[:, :],
                                                 op0=ALU.mult, op1=ALU.mult).then_inc(a_evac, 1)
                    else:
                        dve.tensor_tensor(dst, src, R[:, T - cols:T], ALU.mult).then_inc(a_evac, 1)
                    dve_split(dve, P + j + RING)

                def conv_taps(count):
                    for _ in range(count):
                        i = state["tap"]
                        if i == taps:
                            return
                        state["tap"] += 1
                        c, k = i % CH, i // CH
                        if k == 0:
                            dve.wait_ge(cin_done, CH * l + c + 1)
                            dve.tensor_scalar(cacc[:, c, W2], cpad[:, c, f0:T], conv_w(l, c, 0),
                                              conv_w(l, c, CONV_K), ALU.mult, ALU.add).then_inc(tap_done, 1)
                        else:
                            dve.wait_ge(tap_done, taps * l + i - CH + 1)
                            dve.scalar_tensor_tensor(out=cacc[:, c, W2], in0=cpad[:, c, f0 + k:k + T],
                                                     scalar=conv_w(l, c, k), in1=cacc[:, c, W2],
                                                     op0=ALU.mult, op1=ALU.add).then_inc(tap_done, 1)

                dve.wait_ge(R_ready, y + 1)
                for j in range(20):
                    read_out(j)
                    if 5 <= j < 9:
                        c = j - 5
                        dve.wait_ge(b_gate, CH * l + c + 1)
                        dve.wait_ge(pad_done, l + 1)
                        dve.tensor_tensor(cpad[:, c, CPAD:CPAD + T], proj[:, B_SLOT + c, :],
                                          proj[:, A_SLOT + c, :], ALU.mult).then_inc(cin_done, 1)
                    if 9 <= j < 17:
                        i = j - 9
                        hi, lo = (8 + i, 12 + i) if i < 4 else (i - 4, i)
                        dve.wait_ge(qk_hi_ready, 8 * l + i + 1)
                        dve.tensor_tensor(qk[:, lo, :], proj[:, PLACE[8 + i], :], qk[:, hi, :],
                                          ALU.subtract).then_inc(qk_ready, 1)
                    if j >= 9:
                        conv_taps(TAPS_AT)
                for t in range(SB_HEADS + 3):
                    par = t % 2
                    if t >= 3:
                        hd = t - 3
                        rows = slice(64 * (hd % 2), 64 * (hd % 2) + 64)
                        dve.wait_ge(ao_hi_ready, H + hd + 1)
                        dve.tensor_tensor(ao_lo[rows, hd // 2, :], bank[5][rows, 0:T], ao_hi[rows, hd // 2, :],
                                          ALU.subtract).then_inc(ao_ready, 1)
                    if t < SB_HEADS:
                        read_out(20 + 2 * t)
                    if t == 0:
                        for i, bk in enumerate((4, 5, 7)):
                            dve.wait_ge(v_hi_ready, 3 * l + i + 1)
                            dve.tensor_tensor(v_lo[:, i, :], bank[bk][:, :], v_hi[:, i, :],
                                              ALU.subtract).then_inc(v_ready, 1)
                    if t < SB_HEADS:
                        dve.wait_ge(l_done, H + t + 1)
                        if t >= 1:
                            dve.wait_ge(lk_ready, H + t)
                        if t >= 2:
                            dve.wait_ge(arg_done, H + t - 1)
                        dve.scalar_tensor_tensor(out=nlk[:, :], in0=bank[6][:, 0:SW], scalar=0.0, in1=ez[:, :],
                                                 op0=ALU.max, op1=ALU.add).then_inc(nlk_done, 1)
                        dve.scalar_tensor_tensor(out=ls[:, par, :], in0=bank[6][:, 0:SW], scalar=0.0,
                                                 in1=ez[:, :], op0=ALU.min, op1=ALU.subtract).then_inc(ls_done, 1)
                        conv_taps(TAPS_AT)
                    if 1 <= t <= SB_HEADS:
                        dve.wait_ge(c_full, H + t)
                        dve.wait_ge(ls_done, H + t)
                        if t >= 2:
                            dve.wait_ge(at_ready, H + t - 1)
                        dve.tensor_tensor(ex[:, :], ls[:, 1 - par, :], bank[4][:, 0:SW],
                                          ALU.subtract).then_inc(arg_done, 1)
                    if t < SB_HEADS:
                        read_out(21 + 2 * t)
                        dve.wait_ge(lk_hi_ready, H + t + 1)
                        dve.tensor_tensor(lk_lo[:, :], nlk[:, :], lk_hi[:, :], ALU.subtract).then_inc(lk_ready, 1)
                        conv_taps(TAPS_AT)
                    if 1 <= t <= SB_HEADS:
                        dve.wait_ge(at_hi_ready, H + t)
                        dve.tensor_tensor(at_lo[:, 1 - par, :], ex[:, :], at_hi[:, 1 - par, :],
                                          ALU.subtract).then_inc(at_ready, 1)
                assert state["tap"] == taps
                dve.wait_ge(mu_full, l + 1)
                for c in range(CH):
                    dve.wait_ge(tap_done, taps * (l + 1))
                    dve.tensor_tensor(cacc[:, c, W2], cacc[:, c, W2], bank[7][:, 0:N2], ALU.subtract).then_inc(yc_done, 1)

                def attn_out(p):
                    dve.wait_ge(panel_used, P + 36 + p + 1)
                    for f in (2 * p, 2 * p + 1):
                        dve.wait_ge(gate_done, 2 * l + 1)
                        dve.tensor_tensor(proj[:, G_SLOT + f, W2], proj[:, G_SLOT + f, W2],
                                          bank[(A + 36 + f) % 4][:, 0:N2], ALU.mult).then_inc(a_evac, 1)
                    dve_split(dve, P + 36 + p + RING)

                attn_out(0)
                attn_out(1)
                dve.wait_ge(r2_done, l + 1)
                for c in range(CH):
                    dve.wait_ge(yc_done, CH * l + c + 1)
                    dve.tensor_tensor(cacc[:, c, W2], cacc[:, c, W2], sq[:, W2], ALU.mult).then_inc(yn_done, 1)
                for c in range(CH):
                    dve.wait_ge(co_hi_ready, CH * l + c + 1)
                    dve.tensor_tensor(u_lo[:, c, W2], cacc[:, c, W2], u_hi[:, c, W2], ALU.subtract).then_inc(co_ready, 1)
                attn_out(2)
                attn_out(3)
                for p in range(4):
                    dve.wait_ge(panel_used, P + 40 + p + 1)
                    for f in (2 * p, 2 * p + 1):
                        gc, m = proj[:, G_SLOT + KD + f, W2], proj[:, G_SLOT + f, W2]
                        dve.wait_ge(gate_done, 2 * l + 2)
                        dve.tensor_tensor(gc, gc, bank[(A + 44 + f) % 4][:, 0:N2], ALU.mult).then_inc(a_evac, 1)
                        dve.wait_ge(a_evac, A + 44 + f + 1)
                        dve.tensor_tensor(m, m, gc, ALU.add).then_inc(m_done, 1)
                    dve_split(dve, P + 40 + p + RING)
                    for f in (2 * p, 2 * p + 1):
                        dve.wait_ge(m_hi_ready, KD * l + f + 1)
                        dve.tensor_tensor(qk[:, KD + f, W2], proj[:, G_SLOT + f, W2], qk[:, f, W2],
                                          ALU.subtract).then_inc(m_ready, 1)
                out_proj(y, P + 44, 1, 1.0, N2)

            def da(y):
                b = BASE[y]
                P, A, W = b["P"], b["A"], win(y)
                slopes = [2.0 ** (-8.0 * (i + 1) / DA_HEADS) for i in range(DA_HEADS)]
                dve.wait_ge(lam_step, 5)
                dve.wait_ge(R_ready, y + 1)

                def read_out(j, dst):
                    dve.wait_ge(panel_used, P + j + 1)
                    dve.tensor_tensor(dst, bank[j % 2][:, 0:SEQ], R[:, W], ALU.mult).then_inc(a_evac, 1)
                    dve_split(dve, P + j + RING)

                for t in range(DA_HEADS + 3):
                    if t < DA_HEADS:
                        read_out(3 * t, dqk[:, t % 2, 0, :])
                    if t >= 3:
                        dve.wait_ge(d_av_full, t - 2)
                        dve.tensor_copy(do_[:, :], bank[3][:, 0:SEQ]).then_inc(d_o_done, 1)
                    if 1 <= t <= DA_HEADS:
                        hd = t - 1
                        dve.wait_ge(d_v_hi, hd + 1)
                        dve.tensor_tensor(dv_lo[:, hd % 2, :], bank[2][:, 0:SEQ], dv_hi[:, hd % 2, :],
                                          ALU.subtract).then_inc(d_v_ready, 1)
                        dve.wait_ge(d_rq_done, hd + 1)
                        for i, g in enumerate((q_gain, k_gain)):
                            dve.scalar_tensor_tensor(out=dn[:, i, :], in0=dqk[:, hd % 2, i, :], scalar=g,
                                                     in1=drq[:, i, :], op0=ALU.mult,
                                                     op1=ALU.mult).then_inc(d_n_done, 1)
                    if t < DA_HEADS:
                        read_out(3 * t + 1, dqk[:, t % 2, 1, :])
                    if 1 <= t <= DA_HEADS:
                        dve.wait_ge(d_n_hi, hd + 1)
                        dve.tensor_tensor(dn_lo[:, :, :], dn[:, :, :], dn_hi[:, :, :], ALU.subtract).then_inc(d_n_ready, 1)
                    if 2 <= t <= DA_HEADS + 1:
                        hd = t - 2
                        dve.wait_ge(d_exps, 4 * (hd + 1))
                        dve.reciprocal(dst[:, 12:16], dst[:, 8:12]).then_inc(d_rec, 1)
                        dve.wait_ge(d_rec, hd + 1)
                        dve.tensor_scalar(dst[:, 13:16:2], dst[:, 13:16:2], lam2[:, 2:3], None,
                                          ALU.mult).then_inc(d_c1, 1)
                        dve.wait_ge(d_c1, hd + 1)
                        for i, (c0, w) in enumerate(((0, 128), (128, 256))):
                            dve.tensor_scalar(dt1[:, c0:c0 + w], dp[:, 1, c0:c0 + w], dst[:, 13 + 2 * i:14 + 2 * i],
                                              None, ALU.mult).then_inc(d_t1, 1)
                        for i, (c0, w) in enumerate(((0, 128), (128, 256))):
                            dve.wait_ge(d_t1, 2 * hd + i + 1)
                            dve.scalar_tensor_tensor(out=da_[:, c0:c0 + w], in0=dp[:, 0, c0:c0 + w],
                                                     scalar=dst[:, 12 + 2 * i:13 + 2 * i], in1=dt1[:, c0:c0 + w],
                                                     op0=ALU.mult, op1=ALU.add).then_inc(d_a_done, 1)
                    if t < DA_HEADS:
                        read_out(3 * t + 2, dv[:, :])
                    if t >= 3:
                        dve.wait_ge(d_ro_done, t - 2)
                        dve.scalar_tensor_tensor(out=don[:, :], in0=do_[:, :], scalar=sub_gain, in1=dro[:, :],
                                                 op0=ALU.mult, op1=ALU.mult).then_inc(d_on_done, 1)
                    if 2 <= t <= DA_HEADS + 1:
                        dve.wait_ge(d_T_hi, t - 1)
                        dve.tensor_tensor(dT_lo[:, :], bank[2][:, 0:384], dT_hi[:, :], ALU.subtract)\
                           .then_inc(d_T_ready, 1)
                    if 1 <= t <= DA_HEADS:
                        hd = t - 1
                        if hd == 0:
                            dve.wait_ge(table_loaded, 16 * 3)
                        dve.wait_ge(d_s_full, hd + 1)
                        for m in range(2):
                            dve.scalar_tensor_tensor(out=dsc[:, m, :], in0=dist[:, :], scalar=-slopes[hd],
                                                     in1=bank[6 + m][:, 0:384], op0=ALU.mult,
                                                     op1=ALU.add).then_inc(d_sc_done, 1)
                        dve.wait_ge(d_sc_done, 2 * (hd + 1))
                        dve.tensor_reduce(dst[:, 0:2], dsc[:, :, 0:128], AX.X, ALU.max).then_inc(d_max_done, 1)
                        dve.tensor_reduce(dst[:, 2:4], dsc[:, :, 128:384], AX.X, ALU.max).then_inc(d_max_done, 1)
                        dve.wait_ge(d_max_done, 2 * (hd + 1))
                        dve.tensor_scalar(dst[:, 4:8], dst[:, 0:4], -1.0, None, ALU.mult).then_inc(d_nmax, 1)
                    if t >= 3:
                        dve.wait_ge(d_y_hi, t - 2)
                        dve.tensor_tensor(dy_lo[:, t - 3, :], don[:, :], dy_hi[:, t - 3, :],
                                          ALU.subtract).then_inc(d_y_ready, 1)
                out_proj(y, P + 24, 1, 1.0, SEQ,
                         [bank[f // 2][:, SEQ * (f % 2):SEQ * (f % 2) + SEQ] if f < RING
                          else bank[4 + f % 2][:, 0:SEQ] for f in range(KD)])

            def rt(y):
                b = BASE[y]
                P, A, W = b["P"], b["A"], win(y)
                dve.wait_ge(R_ready, y + 1)

                def gated(j):
                    dve.wait_ge(r_silu, j + 1)
                    dve.wait_ge(r_on_done, 4 * (j // 4 + 1))
                    dve.tensor_tensor(rp[:, j % 2, :], ro[:, j, :], rsg[:, j % 2, :], ALU.mult).then_inc(r_p_done, 1)

                def gated_lo(j):
                    dve.wait_ge(r_y_hi, j + 1)
                    dve.tensor_tensor(ry_lo[:, j, :], rp[:, j % 2, :], ry_hi[:, j, :], ALU.subtract).then_inc(r_y_ready, 1)

                for t in range(RT_HEADS + 2):
                    for c in range(8):
                        j = 8 * (t - RT_HEADS) + c
                        src = bank[c % 2][:, 0:SEQ]
                        dve.wait_ge(panel_used, P + 8 * t + c + 1)
                        if t >= RT_HEADS:
                            dve.tensor_tensor(rg[:, c % 2, :], src, R[:, W], ALU.mult).then_inc(a_evac, 1)
                        elif c >= 4:
                            dve.tensor_tensor(rv[:, c - 4, :], src, R[:, W], ALU.mult).then_inc(a_evac, 1)
                        else:
                            dve.scalar_tensor_tensor(out=rqk[:, t % 2, c, :], in0=src,
                                                     scalar=1.0 if c < 2 else 256 ** -0.5, in1=R[:, W],
                                                     op0=ALU.mult, op1=ALU.mult).then_inc(a_evac, 1)
                        if j >= 1:
                            gated(j - 1)
                        dve_split(dve, P + 8 * t + c + RING)
                        if j >= 1:
                            gated_lo(j - 1)
                        if t < RT_HEADS and c == 4:
                            dve.wait_ge(r_qk_hi, t + 1)
                            dve.tensor_tensor(rqk_lo[:, t % 2, :, :], rqk[:, t % 2, :, :], rqk_hi[:, t % 2, :, :],
                                              ALU.subtract).then_inc(r_qk_ready, 1)
                        if 2 <= t and c == norm_step(t):
                            hd = t - 2
                            dve.wait_ge(r_ro_done, hd + 1)
                            for f in range(4 * hd, 4 * hd + 4):
                                dve.scalar_tensor_tensor(out=ro[:, f, :], in0=ro[:, f, :], scalar=rt_gain(f), in1=rro[:, :],
                                                         op0=ALU.mult, op1=ALU.mult).then_inc(r_on_done, 1)
                        if not 1 <= t <= RT_HEADS:
                            continue
                        hd = t - 1
                        if c == 1:
                            for i in range(2):
                                dve.wait_ge(r_v_hi, 2 * hd + i + 1)
                                dve.tensor_tensor(rv_lo[:, i, :], bank[2 + i][:, :], rv_hi[:, i, :],
                                                  ALU.subtract).then_inc(r_v_ready, 1)
                        if c == 2:
                            dve.wait_ge(r_s_full, hd + 1)
                            dve.wait_ge(r_dec, hd + 1)
                            dve.tensor_tensor(rat[:, :], bank[6][:, 0:384], rdec[:, :], ALU.mult).then_inc(r_at_done, 1)
                        if c == 3:
                            dve.wait_ge(r_at_hi, hd + 1)
                            dve.tensor_tensor(rat_lo[:, :], rat[:, :], rat_hi[:, :], ALU.subtract).then_inc(r_at_ready, 1)
                        if c == 5:
                            dve.wait_ge(r_av_full, hd + 1)
                            for i in range(2):
                                at = 4 * hd + 2 * i
                                dve.tensor_copy(ro[:, at:at + 2, :].rearrange("p a t -> p (a t)"),
                                                bank[4 + i][:, :]).then_inc(r_o_done, 1)
                gated(15)
                gated_lo(15)
                out_proj(y, P + 48, 2, 1.0, SEQ)

            layer = 0
            for y, kind in enumerate(PHASES):
                if kind == "ffn":
                    ffn(y)
                elif kind == "mix":
                    mix(y, layer)
                    layer += 1
                elif kind == "final":
                    dve.tensor_tensor(lam_p[:, :, :], lam_in[:, 0:4:2, :], lam_in[:, 1:4:2, :], ALU.mult)\
                       .then_inc(lam_step, 1)
                    dve.wait_ge(lam_step, 1)
                    dve.tensor_reduce(lam2[:, 0:2], lam_p[:, :, :], AX.X, ALU.add).then_inc(lam_step, 1)
                    dve.tensor_scalar(sub_gain, sub_raw, 1.0 - LAM_INIT, None, ALU.mult).then_inc(lam_step, 1)
                    dve.tensor_scalar(q_gain, q_raw, 64 ** -0.5, None, ALU.mult).then_inc(lam_step, 1)
                    dve.wait_ge(R_ready, y + 1)
                    for f in range(KD):
                        dve.scalar_tensor_tensor(out=h[:, f, META:T], in0=h[:, f, META:T], scalar=gain[:, y, f:f + 1],
                                                 in1=R[:, META:T], op0=ALU.mult, op1=ALU.mult).then_inc(h_done, 1)
                        if f >= 1:
                            dve_update(dve, y + 1, f - 1)
                    dve_update(dve, y + 1, KD - 1)
                    dve.wait_ge(lam_exp, 1)
                    dve.scalar_tensor_tensor(out=lam2[:, 2:3], in0=lam2[:, 1:2], scalar=LAM_INIT, in1=lam2[:, 0:1],
                                             op0=ALU.subtract, op1=ALU.subtract).then_inc(lam_step, 1)
                elif kind == "da":
                    da(y)
                else:
                    rt(y)


        @block.gpsimd
        def _(pool):
            pool.dma_start(consts[:, 1:7, :], cst[:, 128:7 * 128].rearrange("p (a c) -> p a c", c=128))\
                .then_inc(const_loaded, 16)
            pool.dma_start(sgain[:, :], small[:, GAINS:GAINS + SMALLS]).then_inc(const_loaded, 16)
            pool.dma_start(lam_in[:, :, :], lam.partition_broadcast(128)).then_inc(const_loaded, 16)
            pool_update(pool, 0)
            layer = 0
            tables = 0
            for y, kind in enumerate(PHASES):
                if kind in ("mix", "da", "rt"):
                    pool.wait_ge(panel_used, BASE[y]["P"])
                    at = {"mix": 7 * 128, "da": 7 * 128 + SW, "rt": 7 * 128 + SW + 384}[kind]
                    dst = {"mix": smask, "da": dist, "rt": rdist}[kind]
                    w = SW if kind == "mix" else 384
                    pool.dma_start(dst[:, :], cst[:, at:at + w]).then_inc(table_loaded, 16)
                    tables += 1
                if kind == "mix":
                    l, H, W2 = layer, SB_HEADS * layer, win(y + 1)
                    layer += 1
                    pool.memset(cpad[:, :, 0:CPAD], 0.0).then_inc(pad_done, 1)
                    pool.wait_ge(table_loaded, 16 * tables)
                    for t in range(SB_HEADS + 1):
                        if t < SB_HEADS:
                            pool.wait_ge(nlk_done, H + t + 1)
                            pool.tensor_tensor(nlk[:, :], nlk[:, :], smask[:, :], ALU.mult).then_inc(nlk_masked, 1)
                        if t >= 1:
                            pool.wait_ge(ex_done, H + t)
                            pool.tensor_tensor(ex[:, :], ex[:, :], smask[:, :], ALU.mult).then_inc(ex_masked, 1)
                    pool.wait_ge(tap_done, CH * CONV_K * (l + 1))
                    for c in range(1, CH):
                        if c > 1:
                            pool.wait_ge(ysum_step, 3 * l + c - 1)
                        pool.tensor_tensor(sq[:, W2], sq[:, W2] if c > 1 else proj[:, A_SLOT, W2],
                                           proj[:, A_SLOT + c, W2], ALU.add).then_inc(ysum_step, 1)
                if y + 1 < len(PHASES):
                    pool_update(pool, y + 1)


GAINS = len(PHASES) * KD
SMALLS = 2 * CH * (CONV_K + 3) + 3 + 16
CONST_LOADS = 3


def tables():
    p = np.arange(128)[:, None]
    c = np.arange(128)[None, :]
    one = np.ones((128, 128))
    parts = [one / D, one / 512, one / 128, (p // 64 == c // 64) / 64.0, p == c, one, p > c]
    parts += [(np.arange(w)[None, :] - p > 0) for _, _, w in S_TILES]
    far = 1e30
    for d in (p - c, 128 + p - np.arange(256)[None, :],
              np.arange(256)[None, :] - p, c - p):
        parts.append(np.where(d >= 0, d, far))
    return np.ascontiguousarray(np.concatenate([np.asarray(x, np.float64) for x in parts], 1), np.float32)


def kernel(**inputs):
    import numpy as _np
    import concourse.bacc as _bacc
    from concourse import mybir as _mybir
    from concourse.bass_utils import run_bass_kernel_spmd as _run

    x = {k: _np.asarray(v) for k, v in inputs.items()}

    def panels(w, tiles):
        K, F = w.shape
        parts = K // 128 // tiles
        return w.reshape(parts, tiles, 128, F // 128, 128).transpose(3, 0, 2, 1, 4)            .reshape(F // 128 * parts, 128, tiles * 128)

    def pairs(w):
        q = panels(w, 4)
        return q.reshape(q.shape[0] // 2, 2, 128, 512).transpose(0, 2, 1, 3).reshape(-1, 128, 1024)

    p8, p11 = [], []

    def feed_forward(gate, up, down):
        p8.append(_np.stack([panels(gate, 8), panels(up, 8)], 1).reshape(-1, 128, K8))
        p11.append(panels(down, HALF))

    for l in range(2):
        feed_forward(x["ffn1_w_gate"][l], x["ffn1_w_up"][l], x["ffn1_w_down"][l])
        w = panels(x["w_in"][l], 8)
        p8.append(w[[*range(12, 20), *range(0, 12), *range(20, 36)]])
        p8.extend([pairs(x["w_attn_out"][l]), pairs(x["w_conv_out"][l]), panels(x["w_out"][l], 8)])
        feed_forward(x["ffn2_w_gate"][l], x["ffn2_w_up"][l], x["ffn2_w_down"][l])
    for l in range(2):
        w = x["ffn1_w_in_2"][l]
        feed_forward(w[:, :FF], w[:, FF:], x["ffn1_w_out_2"][l])
        if l == 0:
            w = panels(x["da_w_in_2"][0], 8)
            p8.append(w.reshape(3, DA_HEADS, 128, K8).transpose(1, 0, 2, 3).reshape(24, 128, K8))
            p8.append(panels(x["da_w_out_2"][0], 8))
        else:
            w = panels(x["rt_w_in_2"][0], 8)
            order = [t for h in range(RT_HEADS) for t in (2 * h, 2 * h + 1, 8 + 2 * h, 9 + 2 * h, *range(16 + 4 * h, 20 + 4 * h))]
            p8.append(w[order + list(range(32, 48))])
            p8.append(panels(x["rt_w_out_2"][0], 8))
        w = x["ffn2_w_in_2"][l]
        feed_forward(w[:, :FF], w[:, FF:], x["ffn2_w_out_2"][l])

    def column(v):
        return v.reshape(-1, 128).T

    small = [column(x[n][l]) for l in range(2) for n in ("ffn1_norm", "mix_norm", "ffn2_norm")]
    small.append(column(x["final_norm"]))
    small += [column(x[n][l]) for l in range(2) for n in ("ffn1_norm_2", "mix_norm_2", "ffn2_norm_2")]
    for l in range(2):
        per = [column(x["conv_w"][l][k]) for k in range(CONV_K)]
        per += [column(x[n][l]) for n in ("conv_b", "conv_ln_g", "conv_ln_b")]
        small.append(_np.stack(per, 2).reshape(128, -1))
    small += [_np.tile(x["da_q_gain_2"][0], 2)[:, None], _np.tile(x["da_k_gain_2"][0], 2)[:, None],
              x["da_subln_2"][0][:, None], column(x["rt_subln_2"][0])]
    arrays = {
        "w8": _np.concatenate(p8),
        "w11": _np.concatenate(p11),
        "xT": _np.ascontiguousarray(_np.concatenate([x["meta"], x["x"][0]]).T),
        "small": _np.ascontiguousarray(_np.concatenate(small, 1)),
        "cst": tables(),
        "lam": _np.ascontiguousarray(x["da_lambda_2"][0]),
    }
    nc = _bacc.Bacc("TRN2", target_bir_lowering=False, num_devices=1)
    args = [nc.dram_tensor(n, a.shape, _mybir.dt.from_np(a.dtype), kind="ExternalInput").ap() for n, a in arrays.items()]
    out = nc.dram_tensor("outT", (D, SEQ), _mybir.dt.float32, kind="ExternalOutput").ap()
    build(nc, *args, out)
    r = _run(nc, [arrays], core_ids=[0])
    return _np.ascontiguousarray(_np.asarray(r.results[0]["outT"]).T)[None]
```

```python
import math
from contextlib import ExitStack

import numpy as np
import concourse.bass as bass
from concourse import mybir

D = 1024
KD = D // 128
META = 16
SEQ = 256
T = META + SEQ
FF = 2816
FT = FF // 128
HALF = FT // 2
K8 = KD * 128
K11 = HALF * 128
RING = 4
CONV_K = 31
CH = 4
SB_HEADS = 8
DA_HEADS = 8
RT_HEADS = 4
LAM_INIT = 0.8 - 0.6 * math.exp(0.0)
RMS_EPS = 1e-6
LN_EPS = 1e-5

PHASES = ["ffn", "mix", "ffn", "ffn", "mix", "ffn", "final", "ffn", "da", "ffn", "ffn", "rt", "ffn"]
FINAL = PHASES.index("final")
LAST_MIX = FINAL - 2
STREAM = {
    "ffn": [(2 * FT, K8), (2 * KD, K11)],
    "mix": [(36, K8), (8, K8), (8, K8)],
    "da": [(24, K8), (8, K8)],
    "rt": [(48, K8), (16, K8)],
    "final": [],
}
ACCS = {"ffn": 2 * FT, "mix": 36 + 16, "da": 24, "rt": 48, "final": 0}


def bases():
    out, p, p8, p11, a, f = [], 0, 0, 0, 0, 0
    for kind in PHASES:
        out.append(dict(P=p, P8=p8, P11=p11, A=a, F=f))
        for count, cols in STREAM[kind]:
            p += count
            if cols == K8:
                p8 += count
            else:
                p11 += count
        a += ACCS[kind]
        f += FT if kind == "ffn" else 0
    return out, p, p8, p11


BASE, PANELS, PANELS8, PANELS11 = bases()
COLS = [c for kind in PHASES for count, c in STREAM[kind] for _ in range(count)]


LN_EXP, SILU = "natural_log_exp_and_others", "silu_and_others"


def first_col(y):
    return 0 if y <= LAST_MIX else META


def u_base(y):
    return KD * (y if y <= FINAL else y - 1)


S_TILES = [(0, 0, T), (128, T, T - 128), (256, T + T - 128, T - 256)]
SW = S_TILES[2][1] + S_TILES[2][2]
PLACE = [*range(12, 20), *range(4, 12), *range(0, 4), *range(28, 36), *range(20, 28)]
A_SLOT, B_SLOT, V_SLOT, Q_SLOT, K_SLOT, G_SLOT = 12, 16, 0, 4, 8, 20
CPAD = CONV_K - 1
DVE_CONV, DVE_TAPS, DVE_HEAD_TAPS = (0, 1), 2, 3
POOL_CONV, POOL_TAPS, POOL_HEAD_TAPS = (2, 3), 3, 2
FOUR_BANKS = 8 * (RT_HEADS + 1)
TAP_RING = 4
GATES_AT = [1] * 10 + [1, 0, 1, 0, 1, 0, 1, 1, 1, 0]


def gate_panels(half):
    n = sum(GATES_AT[:half])
    return range(20 + n, 20 + n + GATES_AT[half]) if half < len(GATES_AT) else range(0)


def build(nc, w8, w11, xT, small, cst, lam, outT):
    f32 = mybir.dt.float32
    f32r = mybir.dt.float32r
    ALU = mybir.AluOpType
    ACT = mybir.ActivationFunctionType
    AX = mybir.AxisListType
    ctx = ExitStack()

    with ctx:
        def sb(name, shape, dt=f32, where=None):
            return (where or ctx).enter_context(nc.sbuf_tensor(name, shape, dt))

        def sem(name):
            return ctx.enter_context(nc.semaphore(name))

        raw = sb("raw", [128, RING, K11])
        whi = sb("whi", [128, RING, K11], f32r)
        wlo = sb("wlo", [128, RING, K11], f32r)
        h = sb("h", [128, KD, T])
        u_hi = sb("u_hi", [128, KD, T], f32r)
        u_lo = sb("u_lo", [128, KD, T], f32r)
        sq = sb("sq", [128, T])
        ssq = sb("ssq", [128, T])
        R = sb("R", [128, T])
        epsilons = sb("epsilons", [128, 3])
        rms_eps, ln_eps, one = (epsilons[:, i:i + 1] for i in range(3))
        consts = sb("consts", [128, 7, 128])
        mean_d, mean_512, mean_128, mean_64, ident, ones_f, tri_f = (consts[:, i, :] for i in range(7))
        ones_r = sb("ones_r", [128, 128], f32r)
        tri_r = sb("tri_r", [128, 128], f32r)
        gain = sb("gain", [128, len(PHASES), KD])
        both_gains = sb("both_gains", [128, KD])
        sgain = sb("sgain", [128, 2 * CH * (CONV_K + 3) + 3 + 16])
        lam_in = sb("lam_in", [128, 4, 64])
        lam_p = sb("lam_p", [128, 2, 64])
        lam2 = sb("lam2", [128, 5])
        C0 = 2 * CH * (CONV_K + 3)

        def conv_w(l, c, k):
            return sgain[:, (l * CH + c) * (CONV_K + 3) + k:(l * CH + c) * (CONV_K + 3) + k + 1]

        q_raw, k_gain, sub_raw = (sgain[:, C0 + j:C0 + j + 1] for j in range(3))
        q_gain, sub_gain = lam2[:, 3:4], lam2[:, 4:5]

        def rt_gain(j):
            return sgain[:, C0 + 3 + j:C0 + 4 + j]

        with ExitStack() as area:
            hid_hi = sb("hid_hi", [128, FT, T], f32r, area)
            hid_lo = sb("hid_lo", [128, FT, T], f32r, area)
            gt = sb("gt", [128, 2, T], f32, area)
            up = sb("up", [128, 2, T], f32, area)
            sl = sb("sl", [128, 2, T], f32, area)
            pr = sb("pr", [128, 2, T], f32, area)
            R2 = sb("R2", [128, T], f32, area)
            sq2 = sb("sq2", [128, T], f32, area)
        with ExitStack() as area:
            proj = sb("proj", [128, 36, T], f32, area)
            cpad = sb("cpad", [128, CH, CPAD + T], f32, area)
            qk = sb("qk", [128, 16, T], f32r, area)
            v_hi = sb("v_hi", [128, 3, 512], f32r, area)
            v_lo = sb("v_lo", [128, 3, 512], f32r, area)
            ez = sb("ez", [128, SW], f32, area)
            nlk = sb("nlk", [128, SW], f32, area)
            ls = sb("ls", [128, 2, SW], f32, area)
            ex = sb("ex", [128, SW], f32, area)
            lk_hi = sb("lk_hi", [128, SW], f32r, area)
            lk_lo = sb("lk_lo", [128, SW], f32r, area)
            at_hi = sb("at_hi", [128, 2, SW], f32r, area)
            at_lo = sb("at_lo", [128, 2, SW], f32r, area)
            ao_hi = sb("ao_hi", [128, 4, T], f32r, area)
            ao_lo = sb("ao_lo", [128, 4, T], f32r, area)
            smask = sb("smask", [128, SW], f32, area)
            tprod = sb("tprod", [128, TAP_RING, T], f32, area)
        with ExitStack() as area:
            dist = sb("dist", [128, 384], f32, area)
            dqk = sb("dqk", [128, 2, 2, SEQ], f32, area)
            dsq = sb("dsq", [128, 2, SEQ], f32, area)
            drq = sb("drq", [128, 2, SEQ], f32, area)
            dn = sb("dn", [128, 2, SEQ], f32, area)
            dn_hi = sb("dn_hi", [128, 2, SEQ], f32r, area)
            dn_lo = sb("dn_lo", [128, 2, SEQ], f32r, area)
            dv = sb("dv", [128, SEQ], f32, area)
            dv_hi = sb("dv_hi", [128, 2, SEQ], f32r, area)
            dv_lo = sb("dv_lo", [128, 2, SEQ], f32r, area)
            dsc = sb("dsc", [128, 2, 384], f32, area)
            dp = sb("dp", [128, 2, 384], f32, area)
            dst = sb("dst", [128, 16], f32, area)
            dt1 = sb("dt1", [128, 384], f32, area)
            da_ = sb("da_", [128, 384], f32, area)
            dT_hi = sb("dT_hi", [128, 384], f32r, area)
            dT_lo = sb("dT_lo", [128, 384], f32r, area)
            do_ = sb("do_", [128, SEQ], f32, area)
            dosq = sb("dosq", [128, SEQ], f32, area)
            dro = sb("dro", [128, SEQ], f32, area)
            don = sb("don", [128, SEQ], f32, area)
            dy_hi = sb("dy_hi", [128, DA_HEADS, SEQ], f32r, area)
            dy_lo = sb("dy_lo", [128, DA_HEADS, SEQ], f32r, area)
        with ExitStack() as area:
            rdist = sb("rdist", [128, 384], f32, area)
            rqk = sb("rqk", [128, 2, 4, SEQ], f32, area)
            rqk_hi = sb("rqk_hi", [128, 2, 4, SEQ], f32r, area)
            rqk_lo = sb("rqk_lo", [128, 2, 4, SEQ], f32r, area)
            rv = sb("rv", [128, 4, SEQ], f32, area)
            rv_hi = sb("rv_hi", [128, 2, 512], f32r, area)
            rv_lo = sb("rv_lo", [128, 2, 512], f32r, area)
            rdec = sb("rdec", [128, 384], f32, area)
            rat = sb("rat", [128, 384], f32, area)
            rat_hi = sb("rat_hi", [128, 384], f32r, area)
            rat_lo = sb("rat_lo", [128, 384], f32r, area)
            ro = sb("ro", [128, 16, SEQ], f32, area)
            rosq = sb("rosq", [128, 4, SEQ], f32, area)
            rro = sb("rro", [128, SEQ], f32, area)
            rg = sb("rg", [128, 2, SEQ], f32, area)
            rsg = sb("rsg", [128, 2, SEQ], f32, area)
            rp = sb("rp", [128, 2, SEQ], f32, area)
            ry_hi = sb("ry_hi", [128, 16, SEQ], f32r, area)
            ry_lo = sb("ry_lo", [128, 16, SEQ], f32r, area)

        bank = [ctx.enter_context(nc.psum_tensor(f"bank{i}", [128, 512], f32)) for i in range(8)]
        NORM = bank[7]

        raw_loaded = [sem(f"raw_loaded{i}") for i in range(RING)]
        hi_ready, lo_ready, panel_used = sem("hi_ready"), sem("lo_ready"), sem("panel_used")
        a_evac = sem("a_evac")
        h_done, u_hi_ready, u_ready = sem("h_done"), sem("u_hi_ready"), sem("u_ready")
        sq_done, ssq_done = sem("sq_done"), sem("ssq_done")
        norm_full, log_done, R_ready, eps_set = (sem(s) for s in ("norm_full", "log_done", "R_ready", "eps_set"))
        gains_joined, R_joined = sem("gains_joined"), sem("R_joined")
        silu_done, prod_done = sem("silu_done"), sem("prod_done")
        hid_hi_ready, hid_ready = sem("hid_hi_ready"), sem("hid_ready")
        gain_loaded, const_loaded, const_r = (sem(s) for s in ("gain_loaded", "const_loaded", "const_r"))
        x_loaded = [sem(f"x_loaded{i}") for i in range(2)]
        lam_step, lam_exp, table_loaded, stored = (sem(s) for s in ("lam_step", "lam_exp", "table_loaded", "stored"))
        pad_done, b_gate, cin_done, tap_done, tap_product, pool_tap_done = (
            sem(s) for s in ("pad_done", "b_gate", "cin_done", "tap_done", "tap_product", "pool_tap_done"))
        ysum_step, mu_full, yc_done, ysq_done = (sem(s) for s in ("ysum_step", "mu_full", "yc_done", "ysq_done"))
        var_full, r2_done, yn_done, ysilu = (sem(s) for s in ("var_full", "r2_done", "yn_done", "ysilu"))
        co_hi_ready, co_ready, m_done = (sem(s) for s in ("co_hi_ready", "co_ready", "m_done"))
        m_hi_ready, m_ready, gate_done = (sem(s) for s in ("m_hi_ready", "m_ready", "gate_done"))
        r2_log, d_ro_log, d_rq_log, r_ro_log = (
            sem(s) for s in ("r2_log", "d_ro_log", "d_rq_log", "r_ro_log"))
        qk_hi_ready, qk_ready, vt_full, v_hi_ready, v_ready = (
            sem(s) for s in ("qk_hi_ready", "qk_ready", "vt_full", "v_hi_ready", "v_ready"))
        z_full, az_done, e_done, l_done, nlk_done = (
            sem(s) for s in ("z_full", "az_done", "e_done", "l_done", "nlk_done"))
        ls_done, nlk_masked, lk_hi_ready, lk_ready, c_full = (
            sem(s) for s in ("ls_done", "nlk_masked", "lk_hi_ready", "lk_ready", "c_full"))
        arg_done, ex_done, ex_masked, at_hi_ready, at_ready = (
            sem(s) for s in ("arg_done", "ex_done", "ex_masked", "at_hi_ready", "at_ready"))
        o_full, ao_hi_ready, ao_ready = (sem(s) for s in ("o_full", "ao_hi_ready", "ao_ready"))
        d_sq_done, d_qksum, d_rq_done, d_n_done, d_n_hi, d_n_ready = (
            sem(s) for s in ("d_sq_done", "d_qksum", "d_rq_done", "d_n_done", "d_n_hi", "d_n_ready"))
        d_vt_full, d_v_hi, d_v_ready, d_s_full, d_sc_done, d_max_done = (
            sem(s) for s in ("d_vt_full", "d_v_hi", "d_v_ready", "d_s_full", "d_sc_done", "d_max_done"))
        d_nmax, d_exps, d_rec, d_c1, d_t1, d_a_done = (
            sem(s) for s in ("d_nmax", "d_exps", "d_rec", "d_c1", "d_t1", "d_a_done"))
        d_t_full, d_T_hi, d_T_ready, d_av_full, d_o_done, d_osq = (
            sem(s) for s in ("d_t_full", "d_T_hi", "d_T_ready", "d_av_full", "d_o_done", "d_osq"))
        d_osum, d_ro_done, d_on_done, d_y_hi, d_y_ready = (
            sem(s) for s in ("d_osum", "d_ro_done", "d_on_done", "d_y_hi", "d_y_ready"))
        r_vt_full, r_v_hi, r_v_ready, r_qk_hi, r_qk_ready, r_s_full = (
            sem(s) for s in ("r_vt_full", "r_v_hi", "r_v_ready", "r_qk_hi", "r_qk_ready", "r_s_full"))
        r_dec, r_at_done, r_at_hi, r_at_ready, r_av_full, r_o_done = (
            sem(s) for s in ("r_dec", "r_at_done", "r_at_hi", "r_at_ready", "r_av_full", "r_o_done"))
        r_osq, r_osum, r_ro_done, r_on_done = (sem(s) for s in ("r_osq", "r_osum", "r_ro_done", "r_on_done"))
        r_silu, r_p_done, r_y_hi, r_y_ready = (sem(s) for s in ("r_silu", "r_p_done", "r_y_hi", "r_y_ready"))

        block = ctx.enter_context(nc.Block())

        def win(y):
            return slice(first_col(y), T)

        def width(y):
            return T - first_col(y)


        def products(pe, out, slot, k, x_hi, x_lo, first, last):
            w_h, w_l = whi[:, slot, k * 128:k * 128 + 128], wlo[:, slot, k * 128:k * 128 + 128]
            pe.matmul(out, w_h, x_hi, start=first, stop=False)
            pe.matmul(out, w_h, x_lo, start=False, stop=False)
            return pe.matmul(out, w_l, x_hi, start=False, stop=last)

        def act_split(act, n, it=0):
            if not isinstance(it, int) or n < PANELS:
                act.wait_ge(raw_loaded[n % RING], 16 * (n // RING + 1) + 16 * it)
                if n >= RING:
                    act.wait_ge(panel_used, n - RING + 1 + RING * it)
                act.activation(whi[:, n % RING, 0:COLS[n]], raw[:, n % RING, 0:COLS[n]],
                               ACT.Copy).then_inc(hi_ready, 1)

        def dve_split(dve, n, it=0):
            if not isinstance(it, int) or n < PANELS:
                dve.wait_ge(hi_ready, n + 1 + RING * it)
                dve.tensor_tensor(wlo[:, n % RING, 0:COLS[n]], raw[:, n % RING, 0:COLS[n]],
                                  whi[:, n % RING, 0:COLS[n]], ALU.subtract).then_inc(lo_ready, 1)

        def norm_gain(y, f):
            return both_gains[:, f:f + 1] if y == FINAL else gain[:, y, f:f + 1]

        def act_update(act, y, f):
            if y == FINAL + 1 or y == len(PHASES):
                return
            if y == FINAL and f == 0:
                act.wait_ge(gains_joined, 1)
            act.wait_ge(h_done, KD * y + f + 1)
            act.activation(u_hi[:, f, win(y)], h[:, f, win(y)], ACT.Copy,
                           scale=norm_gain(y, f)).then_inc(u_hi_ready, 1)

        def dve_update(dve, y, f):
            if y == FINAL + 1 or y == len(PHASES):
                return
            dve.wait_ge(u_hi_ready, u_base(y) + f + 1)
            dve.scalar_tensor_tensor(out=u_lo[:, f, win(y)], in0=h[:, f, win(y)],
                                     scalar=norm_gain(y, f), in1=u_hi[:, f, win(y)],
                                     op0=ALU.mult, op1=ALU.subtract).then_inc(u_ready, 1)

        def pool_update(pool, y):
            if y == FINAL + 1:
                for f in range(1, KD):
                    pool.wait_ge(sq_done, (KD - 1) * y + f)
                    pool.wait_ge(ssq_done, KD * y + f)
                    pool.tensor_tensor(ssq[:, win(y)], ssq[:, win(y)], (sq, sq2)[f % 2][:, win(y)],
                                       ALU.add).then_inc(ssq_done, 1)
                return
            for f in range(KD):
                pool.wait_ge(h_done, KD * y + f + 1)
                if f == 0:
                    if y > 0:
                        pool.wait_ge(norm_full, y)
                    pool.tensor_tensor(ssq[:, win(y)], h[:, f, win(y)], h[:, f, win(y)],
                                       ALU.mult).then_inc(ssq_done, 1)
                else:
                    pool.wait_ge(ssq_done, KD * y + f)
                    pool.tensor_tensor(sq[:, win(y)], h[:, f, win(y)], h[:, f, win(y)],
                                       ALU.mult).then_inc(sq_done, 1)
                    pool.wait_ge(sq_done, (KD - 1) * y + f)
                    pool.tensor_tensor(ssq[:, win(y)], ssq[:, win(y)], sq[:, win(y)],
                                       ALU.add).then_inc(ssq_done, 1)

        def norm_step(t):
            return 0 if t <= RT_HEADS else 1

        def panel_bank(j):
            return j % (2 if j < FOUR_BANKS else 4)

        def pe_norm(pe, y):
            if y == 0:
                pe.wait_ge(gain_loaded, 32)
            pe.wait_ge(ssq_done, KD * (y + 1))
            pe.matmul(NORM[:, 0:width(y)], mean_d, ssq[:, win(y)],
                      start=True, stop=True).then_inc(norm_full, 1)

        def act_norm(act, y):
            act.preload_act_table_set(LN_EXP)
            act.wait_ge(norm_full, y + 1)
            act_rsqrt(act, (R2 if y == FINAL + 1 else R)[:, win(y)], NORM[:, 0:width(y)], rms_eps, log_done, y + 1, R_ready)

        def act_rsqrt(act, out, src, eps, log_done, count, done):
            act.activation(out, src, ACT.Ln, bias=eps).then_inc(log_done, 1)
            act.wait_ge(log_done, count)
            act.activation(out, out, ACT.Exp, scale=-0.5).then_inc(done, 1)

        def pool_tap(i):
            return POOL_CONV[i % len(POOL_CONV)], i // len(POOL_CONV)


        @block.sync
        def _(sp):
            def load_x(i):
                half = KD // 2
                sp.dma_start(proj[:, half * i:half * i + half, :],
                             xT[D // 2 * i:D // 2 * (i + 1), :].rearrange("(f p) t -> p f t", p=128))\
                  .then_inc(x_loaded[i], 16)

            load_x(0)
            load_x(1)

            def panels(n0, count, src, d0, cols):
                def group(it, empty=False):
                    for j in range(RING):
                        n = n0 + j
                        if not empty:
                            sp.wait_ge(lo_ready, n - RING + 1 + RING * it)
                        sp.dma_start(raw[:, n % RING, 0:cols], src[d0 + j + RING * it, :, :])\
                          .then_inc(raw_loaded[n % RING], 16)
                first = 1 if n0 == 0 else 0
                if first:
                    group(0, empty=True)
                with sp.Fori(first, count // RING) as it:
                    group(it)

            for y, kind in enumerate(PHASES):
                b = BASE[y]
                n, d8 = b["P"], b["P8"]
                for count, cols in STREAM[kind]:
                    if cols == K8:
                        panels(n, count, w8, d8, cols)
                        d8 += count
                    else:
                        panels(n, count, w11, b["P11"], cols)
                    n += count
            for f in range(KD):
                sp.wait_ge(h_done, KD * len(PHASES) + f + 1)
                sp.dma_start(outT[f * 128:f * 128 + 128, :], h[:, f, META:T]).then_inc(stored, 16)
            sp.wait_ge(stored, 16 * KD)


        @block.tensor
        def _(pe):
            def ffn(y):
                b, N, W = BASE[y], width(y), win(y)
                slow = y == 0

                def gate_up(it, norm=False):
                    for j in range(RING):
                        n, g = b["P"] + j, b["A"] + j
                        pe.wait_ge(lo_ready, n + 1 + RING * it)
                        if g + RING * it >= RING if isinstance(it, int) else True:
                            pe.wait_ge(a_evac, g - 3 + RING * it)
                        for k in range(KD):
                            if norm and j == 0 and slow:
                                pe.wait_ge(u_ready, u_base(y) + k + 1)
                            elif norm and j == 0 and k in (0, KD - 2, KD - 1):
                                pe.wait_ge(u_ready, u_base(y) + (KD - 2 if k == 0 else k + 1))
                            mm = products(pe, bank[g % 4][:, 0:N], n % RING, k, u_hi[:, k, W],
                                          u_lo[:, k, W], k == 0, k == KD - 1)
                        mm.then_inc(panel_used, 1)
                        if norm and y == FINAL + 1 and j == 0:
                            pe_norm(pe, FINAL)
                        if norm and j == (3 if y == FINAL + 1 else 1 if slow else 0):
                            if y == FINAL + 1:
                                pe.wait_ge(R_ready, y)
                            pe_norm(pe, y)

                gate_up(0, norm=True)
                with pe.Fori(1, 2 * FT // RING) as it:
                    gate_up(it)
                out_proj(y, b["P"] + 2 * FT, 2, HALF, lambda k: (hid_hi[:, k, W], hid_lo[:, k, W]),
                         hid_ready, b["F"] + FT, N)

            def out_proj(y, n0, per_tile, tiles, x, ready, count, N, lag=3):
                group = RING // per_tile
                with pe.Fori(0, KD // group) as it:
                    for j in range(group):
                        pe.wait_ge(h_done, KD * (y + 1) + j - 1 + group * it)
                        for q in range(per_tile):
                            n = n0 + per_tile * j + q
                            pe.wait_ge(lo_ready, n + 1 + RING * it)
                            for k in range(tiles):
                                K, last = q * tiles + k, per_tile * tiles - 1
                                if j == 0 and (K == 0 or K > last - lag):
                                    pe.wait_ge(ready, count - (lag if K == 0 else last - K))
                                mm = products(pe, bank[4 + j % 2][:, 0:N], n % RING, k, *x(K),
                                              K == 0, K == last)
                            mm.then_inc(panel_used, 1)

            def mix(y, l):
                b = BASE[y]
                P, A = b["P"], b["A"]
                W2, N2 = win(y + 1), width(y + 1)
                flat = qk[:, :, :].rearrange("p a t -> p (a t)")

                def in_panel(j, it=0, cols=T):
                    pe.wait_ge(lo_ready, P + j + 1 + RING * it)
                    pe.wait_ge(a_evac, A + j - 3 + RING * it)
                    for k in range(KD):
                        if j == 0 and isinstance(it, int) and k in (0, KD - 2, KD - 1):
                            pe.wait_ge(u_ready, u_base(y) + (KD - 2 if k == 0 else k + 1))
                        mm = products(pe, bank[(A + j) % 4][:, 0:cols], (P + j) % RING, k, u_hi[:, k, T - cols:T],
                                      u_lo[:, k, T - cols:T], k == 0, k == KD - 1)
                    mm.then_inc(panel_used, 1)

                def scores(hd):
                    if hd == 0:
                        pe.wait_ge(qk_ready, 8 * (l + 1))
                    if hd == 1:
                        pe.wait_ge(v_ready, 3 * (l + 1))
                    if SB_HEADS * l + hd > 1:
                        pe.wait_ge(ls_done, SB_HEADS * l + hd - 1)
                    rows, f = slice(64 * (hd % 2), 64 * (hd % 2) + 64), hd // 2
                    for i, (s0, c0, w) in enumerate(S_TILES):
                        for n, (kt, qt) in enumerate(((0, 8), (0, 12), (4, 8))):
                            ks, qs = (kt + f) * T + s0, (qt + f) * T + s0
                            mm = pe.matmul(bank[6 + hd % 2][:, c0:c0 + w], flat[rows, ks:ks + 128],
                                           flat[rows, qs:qs + w], start=(i == 0 and n == 0),
                                           stop=(n == 2), skip_group_check=True)
                    mm.then_inc(z_full, 1)

                def transpose_v():
                    pe.wait_ge(const_loaded, CONST_LOADS * 16)
                    pe.wait_ge(a_evac, A + 20)
                    vf = proj[:, :, :].rearrange("p a t -> p (a t)")
                    for i, (bk, (s0, _, _)) in enumerate(zip((4, 5, 7), S_TILES)):
                        for f in range(4):
                            at = (V_SLOT + f) * T + s0
                            mm = pe.transpose(bank[bk][:, f * 128:f * 128 + 128], vf[:, at:at + 128], ident)
                        mm.then_inc(vt_full, 1)

                def suffix_sums(hd):
                    pe.wait_ge(lk_ready, SB_HEADS * l + hd + 1)
                    if hd == 0:
                        pe.wait_ge(const_r, 2)
                        pe.wait_ge(v_ready, 3 * (l + 1))
                    else:
                        pe.wait_ge(arg_done, SB_HEADS * l + hd)
                    for n, lk in enumerate((lk_hi, lk_lo)):
                        for i, (s0, c0, w) in enumerate(S_TILES):
                            for i2, (s2, c2, w2) in enumerate(S_TILES[i:]):
                                at = c0 + s2 - s0
                                mm = pe.matmul(bank[4][:, at:at + w2], (ones_r if i2 else tri_r)[:, :],
                                               lk[:, c2:c2 + w2], start=(n == 0 and i == 0 and i2 == 0),
                                               stop=(n == 1), skip_group_check=True)
                    mm.then_inc(c_full, 1)

                def weighted_values(hd):
                    pe.wait_ge(at_ready, SB_HEADS * l + hd + 1)
                    if hd == 0:
                        pe.wait_ge(v_ready, 3 * (l + 1))
                    else:
                        pe.wait_ge(ao_ready, SB_HEADS * l + hd)
                    cols = slice(128 * (hd // 2), 128 * (hd // 2) + 128)
                    for i, (s0, c0, w) in enumerate(S_TILES):
                        for n, (vv, at) in enumerate(((v_hi, at_hi), (v_hi, at_lo), (v_lo, at_hi))):
                            mm = pe.matmul(bank[5][:, s0:T], vv[:, i, cols], at[:, hd % 2, c0:c0 + w],
                                           start=(i == 0 and n == 0), stop=(i == 2 and n == 2),
                                           skip_group_check=True)
                    mm.then_inc(o_full, 1)

                in_panel(0)
                pe_norm(pe, y)
                for j in range(1, 4):
                    in_panel(j)
                with pe.Fori(1, 5) as it:
                    for j in range(RING):
                        in_panel(j, it)
                for t in range(SB_HEADS + 2):
                    if 1 <= t < SB_HEADS:
                        scores(t)
                    if t == SB_HEADS + 1:
                        pe.wait_ge(ysq_done, CH * (l + 1))
                        for c in range(CH):
                            mm = pe.matmul(bank[6][:, 0:N2], mean_512, cpad[:, c, CPAD:CPAD + N2],
                                           start=(c == 0), stop=(c == CH - 1))
                        mm.then_inc(var_full, 1)
                    for j in gate_panels(2 * t):
                        in_panel(j, cols=N2)
                    if t == 0:
                        scores(t)
                        transpose_v()
                    if 1 <= t <= SB_HEADS:
                        suffix_sums(t - 1)
                    if t == SB_HEADS:
                        pe.wait_ge(ls_done, SB_HEADS * (l + 1))
                        pe.wait_ge(ysum_step, 3 * (l + 1))
                        pe.matmul(bank[7][:, 0:N2], mean_512, sq[:, W2], start=True, stop=True).then_inc(mu_full, 1)
                    for j in gate_panels(2 * t + 1):
                        in_panel(j, cols=N2)
                    if t >= 2:
                        weighted_values(t - 2)

                for part in range(2):
                    for p in range(4):
                        n = P + 36 + 4 * part + p
                        pe.wait_ge(lo_ready, n + 1)
                        if p == 0:
                            if part == 1:
                                pe.wait_ge(ao_ready, SB_HEADS * (l + 1))
                        for ff in range(2):
                            g = A + 36 + 8 * part + 2 * p + ff
                            pe.wait_ge(a_evac, g - 3)
                            for k in range(4):
                                if part == 0 and p == 0 and ff == 0:
                                    pe.wait_ge(co_ready, CH * l + k + 1)
                                x_hi, x_lo = ((qk[:, k, W2], qk[:, KD + k, W2]),
                                              (ao_hi[:, k, W2], ao_lo[:, k, W2]))[part]
                                mm = products(pe, bank[g % 4][:, 0:N2], n % RING, 4 * ff + k, x_hi,
                                              x_lo, k == 0, k == 3)
                        mm.then_inc(panel_used, 1)
                out_proj(y, P + 44, 1, KD, lambda k: (qk[:, k, W2], qk[:, KD + k, W2]), m_ready,
                         KD * (l + 1), N2)

            def in_panel2(y, j):
                b = BASE[y]
                pe.wait_ge(lo_ready, b["P"] + j + 1)
                pe.wait_ge(a_evac, b["A"] + j - (1 if j < FOUR_BANKS + 2 else 3))
                for k in range(KD):
                    if j == 0 and k in (0, KD - 2, KD - 1):
                        pe.wait_ge(u_ready, u_base(y) + (KD - 2 if k == 0 else k + 1))
                    mm = products(pe, bank[panel_bank(j)][:, 0:SEQ], (b["P"] + j) % RING, k, u_hi[:, k, META:T],
                                  u_lo[:, k, META:T], k == 0, k == KD - 1)
                mm.then_inc(panel_used, 1)

            def da(y):
                b = BASE[y]

                def out_tiles(f0, f1, k0, k1):
                    if k0 == 0:
                        pe.wait_ge(a_evac, b["A"] + 24)
                    pe.wait_ge(d_y_ready, k1)
                    for f in range(f0, f1):
                        n = b["P"] + 24 + f
                        if k0 == 0:
                            pe.wait_ge(lo_ready, n + 1)
                        for k in range(k0, k1):
                            first = f % 2 == 0 and k == 0
                            w_h, w_l = (w[:, n % RING, k * 128:k * 128 + 128] for w in (whi, wlo))
                            for i, (w, x) in enumerate(((w_h, dy_hi), (w_h, dy_lo), (w_l, dy_hi))):
                                mm = pe.matmul(bank[f // 2][:, SEQ * (f % 2):SEQ * (f % 2) + SEQ], w, x[:, k, :],
                                               start=(first and i == 0), stop=(k == KD - 1 and i == 2),
                                               skip_group_check=True)
                        if k1 == KD:
                            mm.then_inc(panel_used, 1)

                for t in range(DA_HEADS + 3):
                    if t < DA_HEADS:
                        in_panel2(y, 3 * t)
                    if t == 0:
                        pe_norm(pe, y)
                    if 1 <= t <= DA_HEADS:
                        pe.wait_ge(d_sq_done, 2 * t)
                        pe.matmul(bank[4][:, :], mean_64, dsq[:, :, :].rearrange("p a t -> p (a t)"),
                                  start=True, stop=True).then_inc(d_qksum, 1)
                    if t >= 3:
                        hd = t - 3
                        pe.wait_ge(d_T_ready, hd + 1)
                        if hd >= 1:
                            pe.wait_ge(d_o_done, hd)
                        for i, (c0, t0) in enumerate(((0, 0), (256, 128))):
                            for n, (vv, aa) in enumerate(((dv_hi, dT_hi), (dv_hi, dT_lo), (dv_lo, dT_hi))):
                                mm = pe.matmul(bank[3][:, t0:SEQ], vv[:, hd % 2, 128 * i:128 * i + 128],
                                               aa[:, c0:c0 + SEQ - t0], start=(i == 0 and n == 0),
                                               stop=(i == 1 and n == 2), skip_group_check=True)
                        mm.then_inc(d_av_full, 1)
                    if 1 <= t <= DA_HEADS:
                        pe.wait_ge(a_evac, b["A"] + 3 * t)
                        for i in range(2):
                            mm = pe.transpose(bank[2][:, 128 * i:128 * i + 128],
                                              dv[:, 128 * i:128 * i + 128], ident)
                        mm.then_inc(d_vt_full, 1)
                    if t < DA_HEADS:
                        in_panel2(y, 3 * t + 1)
                    elif t == DA_HEADS:
                        out_tiles(0, 2, 0, 5)
                    elif t == DA_HEADS + 1:
                        out_tiles(2, RING, 0, 5)
                    else:
                        out_tiles(0, RING, 6, 7)
                    if t < DA_HEADS:
                        in_panel2(y, 3 * t + 2)
                    if 1 <= t <= DA_HEADS:
                        hd = t - 1
                        pe.wait_ge(d_n_ready, hd + 1)
                        if hd >= 1:
                            pe.wait_ge(d_sc_done, 2 * hd)
                        for m in range(2):
                            rows = slice(64 * m, 64 * m + 64)
                            for i, (c0, w) in enumerate(((0, 128), (128, 256))):
                                for n, (qq, kk) in enumerate(((dn_hi, dn_hi), (dn_hi, dn_lo), (dn_lo, dn_hi))):
                                    mm = pe.matmul(bank[6 + m][:, c0:c0 + w],
                                                   qq[rows, 0, 128 * i:128 * i + 128], kk[rows, 1, 0:w],
                                                   start=(i == 0 and n == 0), stop=(n == 2),
                                                   skip_group_check=True)
                        mm.then_inc(d_s_full, 1)
                    if 2 <= t <= DA_HEADS + 1:
                        pe.wait_ge(d_a_done, 2 * (t - 1))
                        pe.wait_ge(d_v_ready, min(t, DA_HEADS))
                        for dst, src in ((0, 0), (128, 128), (256, 256)):
                            mm = pe.transpose(bank[2][:, dst:dst + 128], da_[:, src:src + 128], ident)
                        mm.then_inc(d_t_full, 1)
                    if t == DA_HEADS + 1:
                        out_tiles(0, RING, 5, 6)
                    if t >= 3:
                        pe.wait_ge(d_osq, t - 2)
                        pe.matmul(bank[5][:, 0:SEQ], mean_128, dosq[:, :], start=True,
                                  stop=True).then_inc(d_osum, 1)
                out_tiles(0, RING, DA_HEADS - 1, DA_HEADS)
                for f in range(RING, KD):
                    n = b["P"] + 24 + f
                    pe.wait_ge(lo_ready, n + 1)
                    if f >= RING + 2:
                        pe.wait_ge(h_done, KD * (y + 1) + f - 1)
                    for k in range(KD):
                        mm = products(pe, bank[4 + f % 2][:, 0:SEQ], n % RING, k, dy_hi[:, k, :], dy_lo[:, k, :],
                                      k == 0, k == KD - 1)
                    mm.then_inc(panel_used, 1)

            def rt(y):
                b = BASE[y]
                for t in range(RT_HEADS + 2):
                    for c in range(8):
                        in_panel2(y, 8 * t + c)
                        if t == 0 and c == 0:
                            pe_norm(pe, y)
                        if not 1 <= t <= RT_HEADS:
                            continue
                        hd = t - 1
                        if c == 0:
                            pe.wait_ge(a_evac, b["A"] + 8 * t)
                            if hd >= 1:
                                pe.wait_ge(r_v_ready, 2 * hd)
                            for i in range(2):
                                for f in range(4):
                                    mm = pe.transpose(bank[2 + i][:, f * 128:f * 128 + 128],
                                                      rv[:, f, 128 * i:128 * i + 128], ident)
                                mm.then_inc(r_vt_full, 1)
                            pe.wait_ge(r_qk_ready, hd + 1)
                            if hd >= 1:
                                pe.wait_ge(r_at_done, hd)
                            p = hd % 2
                            for i, (s0, c0, w) in enumerate(((0, 0, 256), (128, 256, 128))):
                                for f in range(2):
                                    for n, (kk, qq) in enumerate(((rqk_hi, rqk_hi), (rqk_hi, rqk_lo), (rqk_lo, rqk_hi))):
                                        mm = pe.matmul(bank[6][:, c0:c0 + w], kk[:, p, 2 + f, s0:s0 + 128],
                                                       qq[:, p, f, s0:SEQ],
                                                       start=(i == 0 and f == 0 and n == 0),
                                                       stop=(f == 1 and n == 2), skip_group_check=True)
                            mm.then_inc(r_s_full, 1)
                        if c == 4:
                            pe.wait_ge(r_at_ready, hd + 1)
                            pe.wait_ge(r_v_ready, 2 * (hd + 1))
                            if hd >= 1:
                                pe.wait_ge(r_o_done, 2 * hd)
                            for f in range(4):
                                for i, (c0, t0) in enumerate(((0, 0), (256, 128))):
                                    for n, (vv, aa) in enumerate(((rv_hi, rat_hi), (rv_hi, rat_lo), (rv_lo, rat_hi))):
                                        at = 256 * (f % 2) + t0
                                        mm = pe.matmul(bank[4 + f // 2][:, at:at + SEQ - t0],
                                                       vv[:, i, f * 128:f * 128 + 128], aa[:, c0:c0 + SEQ - t0],
                                                       start=(f % 2 == 0 and i == 0 and n == 0),
                                                       stop=(i == 1 and n == 2), skip_group_check=True)
                            mm.then_inc(r_av_full, 1)
                        if c == 7:
                            pe.wait_ge(r_osq, hd + 1)
                            if hd >= 1:
                                pe.wait_ge(r_ro_done, hd)
                            for f in range(4):
                                mm = pe.matmul(bank[7][:, 0:SEQ], mean_512, rosq[:, f, :], start=(f == 0),
                                               stop=(f == 3))
                            mm.then_inc(r_osum, 1)
                out_proj(y, b["P"] + 48, 2, KD, lambda k: (ry_hi[:, k, :], ry_lo[:, k, :]), r_y_ready,
                         16, SEQ, lag=6)

            layer = 0
            for y, kind in enumerate(PHASES):
                if kind == "ffn":
                    ffn(y)
                elif kind == "mix":
                    mix(y, layer)
                    layer += 1
                elif kind == "da":
                    da(y)
                elif kind == "rt":
                    rt(y)


        @block.scalar
        def _(act):
            act.dma_start(gain[:, :, :], small[:, 0:GAINS].rearrange("p (y f) -> p y f", f=KD))\
               .then_inc(gain_loaded, 16)
            act.dma_start(mean_d, cst[:, 0:128]).then_inc(gain_loaded, 16)
            act.preload_act_table_set(LN_EXP)
            act.wait_ge(gain_loaded, 32)
            for f in range(KD):
                act_update(act, 0, f)
                if f == KD - 3:
                    act_split(act, 0)
            for n in range(1, RING):
                act_split(act, n)
            act.wait_ge(eps_set, 3)

            def out_proj(y, n0, per_tile):
                for f in range(KD):
                    if per_tile == 1 and f < KD - 1:
                        act_split(act, n0 + f + RING)
                        act_update(act, y + 1, f)
                        continue
                    act_update(act, y + 1, f)
                    for q in range(per_tile):
                        act_split(act, n0 + per_tile * f + q + RING)

            def ffn(y):
                b, W = BASE[y], win(y)

                act_norm(act, y)

                def pair(it):
                    for p in range(2):
                        f, g, F = 2 * it + p, b["A"] + 2 * p, b["F"] + p
                        act.wait_ge(a_evac, g + 1 + RING * it)
                        act.activation(sl[:, p, W], gt[:, p, W], ACT.Silu).then_inc(silu_done, 1)
                        act_split(act, b["P"] + 2 * p + RING, it)
                        act_split(act, b["P"] + 2 * p + 1 + RING, it)
                        act.wait_ge(prod_done, F + 1 + 2 * it)
                        act.activation(hid_hi[:, f, W], pr[:, p, W], ACT.Copy).then_inc(hid_hi_ready, 1)

                act.preload_act_table_set(SILU)
                with act.Fori(0, FT // 2 - 1) as it:
                    pair(it)
                for p in range(2):
                    f = FT - 2 + p
                    n = b["P"] + 2 * f
                    act.wait_ge(a_evac, b["A"] + 2 * f + 1)
                    act.activation(sl[:, p, W], gt[:, p, W], ACT.Silu).then_inc(silu_done, 1)
                    act_split(act, n + RING)
                    act_split(act, n + 1 + RING)
                    act.wait_ge(prod_done, b["F"] + f + 1)
                    act.activation(hid_hi[:, f, W], pr[:, p, W], ACT.Copy).then_inc(hid_hi_ready, 1)
                out_proj(y, b["P"] + 2 * FT, 2)

            def mix(y, l):
                b = BASE[y]
                P, A, H = b["P"], b["A"], SB_HEADS * l
                W2, N2 = win(y + 1), width(y + 1)
                act_norm(act, y)
                f0, taps, first = T - N2, len(POOL_CONV) * CONV_K, len(POOL_CONV)
                state = {"tap": first}

                def tap_products(count):
                    for i in range(state["tap"], min(state["tap"] + count, taps)):
                        c, k = pool_tap(i)
                        if i < 2 * first:
                            act.wait_ge(cin_done, CH * l + c + 1)
                        m = i - first
                        if m >= TAP_RING:
                            act.wait_ge(pool_tap_done, taps * l + i - TAP_RING + 1)
                        elif l > 0:
                            act.wait_ge(pool_tap_done, taps * l)
                        act.activation(tprod[:, m % TAP_RING, W2], cpad[:, c, f0 + k:k + T], ACT.Copy,
                                       scale=conv_w(l, c, k)).then_inc(tap_product, 1)
                        state["tap"] = i + 1

                for j in range(20):
                    act_split(act, P + j + RING)
                    if 4 <= j < 8:
                        act.wait_ge(a_evac, A + j + 1)
                        act.activation(proj[:, B_SLOT + j - 4, :], proj[:, B_SLOT + j - 4, :],
                                       ACT.Sigmoid).then_inc(b_gate, 1)
                    if 8 <= j < 16:
                        i = j - 8
                        act.wait_ge(a_evac, A + j + 1)
                        act.activation(qk[:, 8 + i if i < 4 else i - 4, :], proj[:, PLACE[j], :],
                                       ACT.Copy).then_inc(qk_hi_ready, 1)
                    if j >= 9:
                        tap_products(POOL_TAPS)
                act.preload_act_table_set(LN_EXP)

                def co_hi(c):
                    act.wait_ge(ysilu, CH * l + c + 1)
                    act.activation(qk[:, c, W2], proj[:, A_SLOT + c, W2], ACT.Copy).then_inc(co_hi_ready, 1)

                for t in range(SB_HEADS + 3):
                    if t < SB_HEADS:
                        act.wait_ge(z_full, H + t + 1)
                        if t >= 1:
                            act.wait_ge(ls_done, H + t)
                        act.activation(ez[:, :], bank[6 + t % 2][:, 0:SW], ACT.Abs).then_inc(az_done, 1)
                        act.wait_ge(az_done, H + t + 1)
                        act.activation(ez[:, :], ez[:, :], ACT.Exp, scale=-1.0).then_inc(e_done, 1)
                        act.wait_ge(e_done, H + t + 1)
                        act.activation(ez[:, :], ez[:, :], ACT.Ln, bias=one).then_inc(l_done, 1)
                    if t >= 3:
                        hd = t - 3
                        rows = slice(64 * (hd % 2), 64 * (hd % 2) + 64)
                        act.wait_ge(o_full, H + hd + 1)
                        act.activation(ao_hi[rows, hd // 2, :], bank[5][rows, 0:T], ACT.Copy)\
                           .then_inc(ao_hi_ready, 1)
                    if t == SB_HEADS + 1:
                        act.wait_ge(var_full, l + 1)
                        act_rsqrt(act, sq[:, W2], bank[6][:, 0:N2], ln_eps, r2_log, l + 1, r2_done)
                        act.preload_act_table_set(SILU)
                        for c in range(CH):
                            act.wait_ge(yn_done, CH * l + c + 1)
                            act.activation(proj[:, A_SLOT + c, W2], proj[:, A_SLOT + c, W2], ACT.Silu,
                                           scale=conv_w(l, c, CONV_K + 1), bias=conv_w(l, c, CONV_K + 2))\
                               .then_inc(ysilu, 1)
                            if c > 0:
                                co_hi(c - 1)
                        co_hi(CH - 1)
                    for j in gate_panels(2 * t):
                        act_split(act, P + j + RING)
                    if t < SB_HEADS:
                        tap_products(POOL_HEAD_TAPS)
                    if t == 0:
                        for i, bk in enumerate((4, 5, 7)):
                            act.wait_ge(vt_full, 3 * l + i + 1)
                            act.activation(v_hi[:, i, :], bank[bk][:, :], ACT.Copy).then_inc(v_hi_ready, 1)
                    if t < SB_HEADS:
                        act.wait_ge(nlk_masked, H + t + 1)
                        if t >= 1:
                            act.wait_ge(c_full, H + t)
                        act.activation(lk_hi[:, :], nlk[:, :], ACT.Copy).then_inc(lk_hi_ready, 1)
                    if 1 <= t <= SB_HEADS:
                        act.wait_ge(arg_done, H + t)
                        act.activation(ex[:, :], ex[:, :], ACT.Exp).then_inc(ex_done, 1)
                    if t == SB_HEADS:
                        for c in range(CH):
                            act.wait_ge(yc_done, CH * l + c + 1)
                            act.activation(cpad[:, c, CPAD:CPAD + N2], proj[:, A_SLOT + c, W2], ACT.Square)\
                               .then_inc(ysq_done, 1)
                    for j in gate_panels(2 * t + 1):
                        act_split(act, P + j + RING)
                    if t < SB_HEADS:
                        tap_products(POOL_HEAD_TAPS)
                    if 1 <= t <= SB_HEADS:
                        hd = t - 1
                        act.wait_ge(ex_masked, H + hd + 1)
                        if hd >= 2:
                            act.wait_ge(o_full, H + hd - 1)
                        act.activation(at_hi[:, hd % 2, :], ex[:, :], ACT.Copy).then_inc(at_hi_ready, 1)
                    if t >= SB_HEADS + 1:
                        g0, count = (G_SLOT + KD, 28) if t == SB_HEADS + 1 else (G_SLOT, 36)
                        act.wait_ge(a_evac, A + count)
                        act.activation(proj[:, g0:g0 + KD, W2], proj[:, g0:g0 + KD, W2], ACT.Sigmoid).then_inc(gate_done, 1)
                for p in range(4):
                    act_split(act, P + 36 + p + RING)
                for p in range(4):
                    if p < 3:
                        act_split(act, P + 40 + p + RING)
                    for f in (2 * p, 2 * p + 1):
                        act.wait_ge(m_done, KD * l + f + 1)
                        act.activation(qk[:, f, W2], proj[:, G_SLOT + f, W2], ACT.Copy).then_inc(m_hi_ready, 1)
                act_split(act, P + 43 + RING)
                out_proj(y, P + 44, 1)

            def da(y):
                b = BASE[y]
                P, A = b["P"], b["A"]
                act_norm(act, y)

                def normed_hi(hd):
                    act.wait_ge(d_on_done, hd + 1)
                    act.activation(dy_hi[:, hd, :], don[:, :], ACT.Copy).then_inc(d_y_hi, 1)

                for t in range(DA_HEADS + 3):
                    if 2 <= t <= DA_HEADS + 1:
                        act.wait_ge(d_nmax, t - 1)
                        for i, (c0, w) in enumerate(((0, 128), (128, 256))):
                            for m in range(2):
                                j = 2 * i + m
                                act.activation(dp[:, m, c0:c0 + w], dsc[:, m, c0:c0 + w], ACT.Exp,
                                               bias=dst[:, 4 + j:5 + j], accum_out=dst[:, 8 + j:9 + j])\
                                   .then_inc(d_exps, 1)
                    if t >= 4:
                        normed_hi(t - 4)
                    if t < DA_HEADS:
                        act_split(act, P + 3 * t + RING)
                    if 1 <= t <= DA_HEADS:
                        act.wait_ge(d_vt_full, t)
                        act.activation(dv_hi[:, (t - 1) % 2, :], bank[2][:, 0:SEQ], ACT.Copy).then_inc(d_v_hi, 1)
                        act.wait_ge(d_qksum, t)
                        act_rsqrt(act, drq[:, :, :].rearrange("p a t -> p (a t)"), bank[4][:, :], rms_eps,
                                  d_rq_log, t, d_rq_done)
                    if t >= 3:
                        act.wait_ge(d_o_done, t - 2)
                        act.activation(dosq[:, :], do_[:, :], ACT.Square).then_inc(d_osq, 1)
                    if 1 <= t <= DA_HEADS:
                        act.wait_ge(d_n_done, 2 * t)
                        act.activation(dn_hi[:, :, :], dn[:, :, :], ACT.Copy).then_inc(d_n_hi, 1)
                    if t < DA_HEADS:
                        act_split(act, P + 3 * t + 1 + RING)
                    if t < DA_HEADS:
                        act_split(act, P + 3 * t + 2 + RING)
                        act.wait_ge(a_evac, A + 3 * t + 2)
                        for i in range(2):
                            act.activation(dsq[:, i, :], dqk[:, t % 2, i, :], ACT.Square).then_inc(d_sq_done, 1)
                    if 2 <= t <= DA_HEADS + 1:
                        act.wait_ge(d_t_full, t - 1)
                        act.activation(dT_hi[:, :], bank[2][:, 0:384], ACT.Copy).then_inc(d_T_hi, 1)
                    if t >= 3:
                        act.wait_ge(d_osum, t - 2)
                        act_rsqrt(act, dro[:, :], bank[5][:, 0:SEQ], rms_eps, d_ro_log, t - 2, d_ro_done)
                normed_hi(DA_HEADS - 1)
                out_proj(y, P + 24, 1)

            def rt(y):
                b = BASE[y]
                P, A = b["P"], b["A"]
                act_norm(act, y)

                def gated_hi(j):
                    act.wait_ge(r_p_done, j + 1)
                    act.activation(ry_hi[:, j, :], rp[:, j % 2, :], ACT.Copy).then_inc(r_y_hi, 1)

                for t in range(RT_HEADS + 2):
                    for c in range(8):
                        j = 8 * (t - RT_HEADS) + c
                        if 2 <= t and c == norm_step(t):
                            act.wait_ge(r_osum, t - 1)
                            act_rsqrt(act, rro[:, :], bank[7][:, 0:SEQ], rms_eps, r_ro_log, t - 1, r_ro_done)
                        if 1 <= t <= RT_HEADS and c == 0:
                            hd = t - 1
                            if hd == 0:
                                act.wait_ge(table_loaded, 16 * 4)
                            else:
                                act.wait_ge(r_at_done, hd)
                            act.activation(rdec[:, :], rdist[:, :], ACT.Exp,
                                           scale=math.log(1.0 - 2.0 ** (-5 - hd))).then_inc(r_dec, 1)
                        act_split(act, P + 8 * t + c + RING)
                        if t >= RT_HEADS:
                            act.wait_ge(a_evac, A + 8 * t + c + 1)
                            act.activation(rsg[:, c % 2, :], rg[:, c % 2, :], ACT.Silu).then_inc(r_silu, 1)
                        if j >= 1:
                            gated_hi(j - 1)
                        if t < RT_HEADS and c == 3:
                            act.wait_ge(a_evac, A + 8 * t + 4)
                            act.activation(rqk_hi[:, t % 2, :, :], rqk[:, t % 2, :, :], ACT.Copy).then_inc(r_qk_hi, 1)
                        if not 1 <= t <= RT_HEADS:
                            continue
                        hd = t - 1
                        if c == 0:
                            for i in range(2):
                                act.wait_ge(r_vt_full, 2 * hd + i + 1)
                                act.activation(rv_hi[:, i, :], bank[2 + i][:, :], ACT.Copy).then_inc(r_v_hi, 1)
                        if c == 1:
                            act.wait_ge(r_at_done, hd + 1)
                            act.activation(rat_hi[:, :], rat[:, :], ACT.Copy).then_inc(r_at_hi, 1)
                        if c == 5:
                            act.wait_ge(r_o_done, 2 * (hd + 1))
                            act.activation(rosq[:, :, :], ro[:, 4 * hd:4 * hd + 4, :], ACT.Square).then_inc(r_osq, 1)
                gated_hi(15)
                out_proj(y, P + 48, 2)

            layer = 0
            for y, kind in enumerate(PHASES):
                if kind == "ffn":
                    ffn(y)
                elif kind == "mix":
                    mix(y, layer)
                    layer += 1
                elif kind == "final":
                    act_norm(act, y)
                    act.wait_ge(lam_step, 2)
                    act.activation(lam2[:, 0:2], lam2[:, 0:2], ACT.Exp).then_inc(lam_exp, 1)
                    for f in range(KD):
                        act.wait_ge(h_done, KD * (y + 1) + f + 1)
                        if f >= 3:
                            act.wait_ge(ssq_done, KD * (y + 1) + f - 1)
                        act.activation((ssq if f == 0 else (sq, sq2)[f % 2])[:, win(y)], h[:, f, win(y)],
                                       ACT.Square).then_inc(sq_done if f else ssq_done, 1)
                elif kind == "da":
                    da(y)
                else:
                    rt(y)


        @block.vector
        def _(dve):
            for tile, value in ((rms_eps, RMS_EPS), (ln_eps, LN_EPS), (one, 1.0)):
                dve.memset(tile, value).then_inc(eps_set, 1)
            dve.wait_ge(gain_loaded, 32)
            half = KD // 2
            for i in range(2):
                dve.wait_ge(x_loaded[i], 16)
                for f in range(half * i, half * i + half):
                    dve.tensor_copy(h[:, f, :], proj[:, f, :]).then_inc(h_done, 1)
                for f in range(half * i, half * i + half):
                    dve_update(dve, 0, f)
                    if f == KD - 3:
                        dve_split(dve, 0)
            for n in range(1, RING):
                dve_split(dve, n)
            dve.tensor_tensor(both_gains[:, :], gain[:, FINAL, :], gain[:, FINAL + 1, :], ALU.mult).then_inc(gains_joined, 1)

            def out_proj(y, n0, per_tile, factor, N, sources=None):
                W = win(y if N == width(y) else y + 1)
                for f in range(KD):
                    src = sources[f] if sources else bank[4 + f % 2][:, 0:N]
                    dve.wait_ge(panel_used, n0 + (f // 2 * 2 + 2 if sources and f < RING else per_tile * (f + 1)))
                    dve.scalar_tensor_tensor(out=h[:, f, W], in0=src, scalar=factor,
                                             in1=h[:, f, W], op0=ALU.mult, op1=ALU.add).then_inc(h_done, 1)
                    if per_tile == 1 and f > 0:
                        dve_update(dve, y + 1, f - 1)
                    if f == KD - 1:
                        dve_update(dve, y + 1, f)
                    for q in range(per_tile):
                        dve_split(dve, n0 + per_tile * f + q + RING)
                        if per_tile == 2 and q == 0 and f < KD - 1:
                            dve_update(dve, y + 1, f)

            def ffn(y):
                b, N, W = BASE[y], width(y), win(y)

                def tile(n, g, F, f, p, it, last):
                    it4, it2 = (RING * it, 2 * it) if not last else (0, 0)
                    dve.wait_ge(panel_used, n + 1 + it4)
                    dve.tensor_tensor(gt[:, p, W], bank[g % 4][:, 0:N], R[:, W], ALU.mult).then_inc(a_evac, 1)
                    dve.wait_ge(panel_used, n + 2 + it4)
                    dve.tensor_tensor(up[:, p, W], bank[(g + 1) % 4][:, 0:N], R[:, W], ALU.mult).then_inc(a_evac, 1)
                    dve_split(dve, n + RING, it)
                    dve.wait_ge(silu_done, F + 1 + it2)
                    dve.wait_ge(a_evac, g + 2 + it4)
                    dve.tensor_tensor(pr[:, p, W], sl[:, p, W], up[:, p, W], ALU.mult).then_inc(prod_done, 1)
                    dve_split(dve, n + 1 + RING, it)
                    dve.wait_ge(hid_hi_ready, F + 1 + it2)
                    dve.tensor_tensor(hid_lo[:, f, W], pr[:, p, W], hid_hi[:, f, W], ALU.subtract)\
                       .then_inc(hid_ready, 1)

                dve.wait_ge(R_ready, y + 1)
                if y == FINAL + 1:
                    dve.tensor_tensor(R[:, W], R[:, W], R2[:, W], ALU.mult).then_inc(R_joined, 1)
                    dve.wait_ge(R_joined, 1)
                with dve.Fori(0, FT // 2 - 1) as it:
                    for p in range(2):
                        tile(b["P"] + 2 * p, b["A"] + 2 * p, b["F"] + p, 2 * it + p, p, it, False)
                for p in range(2):
                    f = FT - 2 + p
                    tile(b["P"] + 2 * f, b["A"] + 2 * f, b["F"] + f, f, p, 0, True)
                out_proj(y, b["P"] + 2 * FT, 2, 0.5, N)

            def mix(y, l):
                b = BASE[y]
                P, A, H = b["P"], b["A"], SB_HEADS * l
                W2, N2 = win(y + 1), width(y + 1)
                cacc = proj[:, A_SLOT:A_SLOT + CH, :]
                state = {"tap": 0}

                def read_out(j):
                    dve.wait_ge(panel_used, P + j + 1)
                    cols = T if j < 20 else N2
                    src, dst = bank[(A + j) % 4][:, 0:cols], proj[:, PLACE[j], T - cols:T]
                    if 8 <= j < 12:
                        dve.scalar_tensor_tensor(out=dst, in0=src, scalar=64 ** -0.5, in1=R[:, :],
                                                 op0=ALU.mult, op1=ALU.mult).then_inc(a_evac, 1)
                    else:
                        dve.tensor_tensor(dst, src, R[:, T - cols:T], ALU.mult).then_inc(a_evac, 1)
                    dve_split(dve, P + j + RING)

                def taps(count):
                    total, f0 = len(DVE_CONV) * CONV_K, T - N2
                    for i in range(state["tap"], min(state["tap"] + count, total)):
                        c, k = DVE_CONV[i % len(DVE_CONV)], i // len(DVE_CONV)
                        if k == 0:
                            dve.wait_ge(cin_done, CH * l + c + 1)
                            dve.tensor_scalar(cacc[:, c, W2], cpad[:, c, f0:T], conv_w(l, c, 0),
                                              conv_w(l, c, CONV_K), ALU.mult, ALU.add).then_inc(tap_done, 1)
                        else:
                            dve.wait_ge(tap_done, total * l + i - len(DVE_CONV) + 1)
                            dve.scalar_tensor_tensor(out=cacc[:, c, W2], in0=cpad[:, c, f0 + k:k + T],
                                                     scalar=conv_w(l, c, k), in1=cacc[:, c, W2],
                                                     op0=ALU.mult, op1=ALU.add).then_inc(tap_done, 1)
                        state["tap"] = i + 1

                if l == 0:
                    dve.wait_ge(const_loaded, CONST_LOADS * 16)
                    dve.tensor_copy(ones_r[:, :], ones_f).then_inc(const_r, 1)
                    dve.tensor_copy(tri_r[:, :], tri_f).then_inc(const_r, 1)
                dve.wait_ge(R_ready, y + 1)
                for j in range(20):
                    read_out(j)
                    if 5 <= j < 9:
                        c = j - 5
                        dve.wait_ge(b_gate, CH * l + c + 1)
                        dve.wait_ge(pad_done, l + 1)
                        dve.tensor_tensor(cpad[:, c, CPAD:CPAD + T], proj[:, B_SLOT + c, :],
                                          proj[:, A_SLOT + c, :], ALU.mult).then_inc(cin_done, 1)
                    if 9 <= j < 17:
                        i = j - 9
                        hi, lo = (8 + i, 12 + i) if i < 4 else (i - 4, i)
                        dve.wait_ge(qk_hi_ready, 8 * l + i + 1)
                        dve.tensor_tensor(qk[:, lo, :], proj[:, PLACE[8 + i], :], qk[:, hi, :],
                                          ALU.subtract).then_inc(qk_ready, 1)
                    if j >= 9:
                        taps(DVE_TAPS)
                for t in range(SB_HEADS + 3):
                    par = t % 2
                    if t >= 3:
                        hd = t - 3
                        rows = slice(64 * (hd % 2), 64 * (hd % 2) + 64)
                        dve.wait_ge(ao_hi_ready, H + hd + 1)
                        dve.tensor_tensor(ao_lo[rows, hd // 2, :], bank[5][rows, 0:T], ao_hi[rows, hd // 2, :],
                                          ALU.subtract).then_inc(ao_ready, 1)
                    if t == SB_HEADS + 1:
                        dve.wait_ge(r2_done, l + 1)
                        for c in range(CH):
                            dve.wait_ge(yc_done, CH * l + c + 1)
                            dve.tensor_tensor(cacc[:, c, W2], cacc[:, c, W2], sq[:, W2], ALU.mult).then_inc(yn_done, 1)
                        for c in range(CH):
                            dve.wait_ge(co_hi_ready, CH * l + c + 1)
                            dve.tensor_tensor(qk[:, KD + c, W2], cacc[:, c, W2], qk[:, c, W2],
                                              ALU.subtract).then_inc(co_ready, 1)
                    for j in gate_panels(2 * t):
                        read_out(j)
                    if t == 0:
                        for i, bk in enumerate((4, 5, 7)):
                            dve.wait_ge(v_hi_ready, 3 * l + i + 1)
                            dve.tensor_tensor(v_lo[:, i, :], bank[bk][:, :], v_hi[:, i, :],
                                              ALU.subtract).then_inc(v_ready, 1)
                    if t < SB_HEADS:
                        dve.wait_ge(l_done, H + t + 1)
                        if t >= 1:
                            dve.wait_ge(lk_ready, H + t)
                        if t >= 2:
                            dve.wait_ge(arg_done, H + t - 1)
                        dve.scalar_tensor_tensor(out=nlk[:, :], in0=bank[6 + par][:, 0:SW], scalar=0.0, in1=ez[:, :],
                                                 op0=ALU.max, op1=ALU.add).then_inc(nlk_done, 1)
                        dve.scalar_tensor_tensor(out=ls[:, par, :], in0=bank[6 + par][:, 0:SW], scalar=0.0,
                                                 in1=ez[:, :], op0=ALU.min, op1=ALU.subtract).then_inc(ls_done, 1)
                        taps(DVE_HEAD_TAPS)
                    if 1 <= t <= SB_HEADS:
                        dve.wait_ge(c_full, H + t)
                        dve.wait_ge(ls_done, H + t)
                        if t >= 2:
                            dve.wait_ge(at_ready, H + t - 1)
                        dve.tensor_tensor(ex[:, :], ls[:, 1 - par, :], bank[4][:, 0:SW],
                                          ALU.subtract).then_inc(arg_done, 1)
                    if t == SB_HEADS:
                        assert state["tap"] == len(DVE_CONV) * CONV_K
                        dve.wait_ge(mu_full, l + 1)
                        dve.wait_ge(tap_done, len(DVE_CONV) * CONV_K * (l + 1))
                        dve.wait_ge(pool_tap_done, len(POOL_CONV) * CONV_K * (l + 1))
                        for c in range(CH):
                            dve.tensor_tensor(cacc[:, c, W2], cacc[:, c, W2], bank[7][:, 0:N2], ALU.subtract)\
                               .then_inc(yc_done, 1)
                    if t < SB_HEADS:
                        dve.wait_ge(lk_hi_ready, H + t + 1)
                        dve.tensor_tensor(lk_lo[:, :], nlk[:, :], lk_hi[:, :], ALU.subtract).then_inc(lk_ready, 1)
                    for j in gate_panels(2 * t + 1):
                        read_out(j)
                    if 1 <= t <= SB_HEADS:
                        dve.wait_ge(at_hi_ready, H + t)
                        dve.tensor_tensor(at_lo[:, 1 - par, :], ex[:, :], at_hi[:, 1 - par, :],
                                          ALU.subtract).then_inc(at_ready, 1)
                    if t < SB_HEADS:
                        taps(DVE_HEAD_TAPS)
                for p in range(4):
                    dve.wait_ge(panel_used, P + 36 + p + 1)
                    for f in (2 * p, 2 * p + 1):
                        gate = proj[:, G_SLOT + KD + f, W2]
                        dve.wait_ge(gate_done, 2 * l + 1)
                        dve.tensor_tensor(gate, gate, bank[(A + 36 + f) % 4][:, 0:N2], ALU.mult).then_inc(a_evac, 1)
                    dve_split(dve, P + 36 + p + RING)
                for p in range(4):
                    dve.wait_ge(panel_used, P + 40 + p + 1)
                    dve.wait_ge(gate_done, 2 * l + 2)
                    for f in (2 * p, 2 * p + 1):
                        m = proj[:, G_SLOT + f, W2]
                        dve.tensor_tensor(m, m, bank[(A + 44 + f) % 4][:, 0:N2], ALU.mult).then_inc(a_evac, 1)
                    for f in (2 * p, 2 * p + 1):
                        m = proj[:, G_SLOT + f, W2]
                        dve.wait_ge(a_evac, A + 44 + f + 1)
                        dve.tensor_tensor(m, m, proj[:, G_SLOT + KD + f, W2], ALU.add).then_inc(m_done, 1)
                    if p < 3:
                        dve_split(dve, P + 40 + p + RING)
                    for f in (2 * p, 2 * p + 1):
                        dve.wait_ge(m_hi_ready, KD * l + f + 1)
                        dve.tensor_tensor(qk[:, KD + f, W2], proj[:, G_SLOT + f, W2], qk[:, f, W2],
                                          ALU.subtract).then_inc(m_ready, 1)
                dve_split(dve, P + 43 + RING)
                out_proj(y, P + 44, 1, 1.0, N2)

            def da(y):
                b = BASE[y]
                P, A, W = b["P"], b["A"], win(y)
                slopes = [2.0 ** (-8.0 * (i + 1) / DA_HEADS) for i in range(DA_HEADS)]
                dve.wait_ge(lam_step, 5)
                dve.wait_ge(R_ready, y + 1)

                def read_out(j, dst):
                    dve.wait_ge(panel_used, P + j + 1)
                    dve.tensor_tensor(dst, bank[j % 2][:, 0:SEQ], R[:, W], ALU.mult).then_inc(a_evac, 1)
                    dve_split(dve, P + j + RING)

                def normed_lo(hd):
                    dve.wait_ge(d_y_hi, hd + 1)
                    dve.tensor_tensor(dy_lo[:, hd, :], don[:, :], dy_hi[:, hd, :],
                                      ALU.subtract).then_inc(d_y_ready, 1)

                for t in range(DA_HEADS + 3):
                    if t < DA_HEADS:
                        read_out(3 * t, dqk[:, t % 2, 0, :])
                    if t >= 4:
                        normed_lo(t - 4)
                    if t >= 3:
                        dve.wait_ge(d_av_full, t - 2)
                        dve.tensor_copy(do_[:, :], bank[3][:, 0:SEQ]).then_inc(d_o_done, 1)
                    if 1 <= t <= DA_HEADS:
                        hd = t - 1
                        dve.wait_ge(d_v_hi, hd + 1)
                        dve.tensor_tensor(dv_lo[:, hd % 2, :], bank[2][:, 0:SEQ], dv_hi[:, hd % 2, :],
                                          ALU.subtract).then_inc(d_v_ready, 1)
                        dve.wait_ge(d_rq_done, hd + 1)
                        for i, g in enumerate((q_gain, k_gain)):
                            dve.scalar_tensor_tensor(out=dn[:, i, :], in0=dqk[:, hd % 2, i, :], scalar=g,
                                                     in1=drq[:, i, :], op0=ALU.mult,
                                                     op1=ALU.mult).then_inc(d_n_done, 1)
                    if 2 <= t <= DA_HEADS + 1:
                        hd = t - 2
                        dve.wait_ge(d_exps, 4 * (hd + 1))
                        dve.reciprocal(dst[:, 12:16], dst[:, 8:12]).then_inc(d_rec, 1)
                        dve.wait_ge(d_rec, hd + 1)
                        dve.tensor_scalar(dst[:, 13:16:2], dst[:, 13:16:2], lam2[:, 2:3], None,
                                          ALU.mult).then_inc(d_c1, 1)
                        dve.wait_ge(d_c1, hd + 1)
                        for i, (c0, w) in enumerate(((0, 128), (128, 256))):
                            dve.tensor_scalar(dt1[:, c0:c0 + w], dp[:, 1, c0:c0 + w], dst[:, 13 + 2 * i:14 + 2 * i],
                                              None, ALU.mult).then_inc(d_t1, 1)
                        for i, (c0, w) in enumerate(((0, 128), (128, 256))):
                            dve.wait_ge(d_t1, 2 * hd + i + 1)
                            dve.scalar_tensor_tensor(out=da_[:, c0:c0 + w], in0=dp[:, 0, c0:c0 + w],
                                                     scalar=dst[:, 12 + 2 * i:13 + 2 * i], in1=dt1[:, c0:c0 + w],
                                                     op0=ALU.mult, op1=ALU.add).then_inc(d_a_done, 1)
                    if 1 <= t <= DA_HEADS:
                        hd = t - 1
                        dve.wait_ge(d_n_hi, hd + 1)
                        dve.tensor_tensor(dn_lo[:, :, :], dn[:, :, :], dn_hi[:, :, :], ALU.subtract).then_inc(d_n_ready, 1)
                    if t < DA_HEADS:
                        read_out(3 * t + 1, dqk[:, t % 2, 1, :])
                    if t < DA_HEADS:
                        read_out(3 * t + 2, dv[:, :])
                    if 1 <= t <= DA_HEADS:
                        hd = t - 1
                        if hd == 0:
                            dve.wait_ge(table_loaded, 16 * 3)
                        dve.wait_ge(d_s_full, hd + 1)
                        for m in range(2):
                            dve.scalar_tensor_tensor(out=dsc[:, m, :], in0=dist[:, :], scalar=-slopes[hd],
                                                     in1=bank[6 + m][:, 0:384], op0=ALU.mult,
                                                     op1=ALU.add).then_inc(d_sc_done, 1)
                        dve.wait_ge(d_sc_done, 2 * (hd + 1))
                        dve.tensor_reduce(dst[:, 0:2], dsc[:, :, 0:128], AX.X, ALU.max).then_inc(d_max_done, 1)
                        dve.tensor_reduce(dst[:, 2:4], dsc[:, :, 128:384], AX.X, ALU.max).then_inc(d_max_done, 1)
                        dve.wait_ge(d_max_done, 2 * (hd + 1))
                        dve.tensor_scalar(dst[:, 4:8], dst[:, 0:4], -1.0, None, ALU.mult).then_inc(d_nmax, 1)
                    if 2 <= t <= DA_HEADS + 1:
                        dve.wait_ge(d_T_hi, t - 1)
                        dve.tensor_tensor(dT_lo[:, :], bank[2][:, 0:384], dT_hi[:, :], ALU.subtract)\
                           .then_inc(d_T_ready, 1)
                    if t >= 3:
                        dve.wait_ge(d_ro_done, t - 2)
                        dve.scalar_tensor_tensor(out=don[:, :], in0=do_[:, :], scalar=sub_gain, in1=dro[:, :],
                                                 op0=ALU.mult, op1=ALU.mult).then_inc(d_on_done, 1)
                normed_lo(DA_HEADS - 1)
                out_proj(y, P + 24, 1, 1.0, SEQ,
                         [bank[f // 2][:, SEQ * (f % 2):SEQ * (f % 2) + SEQ] if f < RING
                          else bank[4 + f % 2][:, 0:SEQ] for f in range(KD)])

            def rt(y):
                b = BASE[y]
                P, A, W = b["P"], b["A"], win(y)
                dve.wait_ge(R_ready, y + 1)

                def normed(f):
                    dve.scalar_tensor_tensor(out=ro[:, f, :], in0=ro[:, f, :], scalar=rt_gain(f), in1=rro[:, :],
                                             op0=ALU.mult, op1=ALU.mult).then_inc(r_on_done, 1)

                def gated(j):
                    dve.wait_ge(r_silu, j + 1)
                    dve.wait_ge(r_on_done, 4 * (j // 4 + 1))
                    dve.tensor_tensor(rp[:, j % 2, :], ro[:, j, :], rsg[:, j % 2, :], ALU.mult).then_inc(r_p_done, 1)

                def gated_lo(j):
                    dve.wait_ge(r_y_hi, j + 1)
                    dve.tensor_tensor(ry_lo[:, j, :], rp[:, j % 2, :], ry_hi[:, j, :], ALU.subtract).then_inc(r_y_ready, 1)

                for t in range(RT_HEADS + 2):
                    for c in range(8):
                        j = 8 * (t - RT_HEADS) + c
                        src = bank[panel_bank(8 * t + c)][:, 0:SEQ]
                        dve.wait_ge(panel_used, P + 8 * t + c + 1)
                        if t >= RT_HEADS:
                            dve.tensor_tensor(rg[:, c % 2, :], src, R[:, W], ALU.mult).then_inc(a_evac, 1)
                        elif c >= 4:
                            dve.tensor_tensor(rv[:, c - 4, :], src, R[:, W], ALU.mult).then_inc(a_evac, 1)
                        else:
                            dve.scalar_tensor_tensor(out=rqk[:, t % 2, c, :], in0=src,
                                                     scalar=1.0 if c < 2 else 256 ** -0.5, in1=R[:, W],
                                                     op0=ALU.mult, op1=ALU.mult).then_inc(a_evac, 1)
                        if j >= 1:
                            gated(j - 1)
                        dve_split(dve, P + 8 * t + c + RING)
                        if j >= 1:
                            gated_lo(j - 1)
                        if t < RT_HEADS and c == 4:
                            dve.wait_ge(r_qk_hi, t + 1)
                            dve.tensor_tensor(rqk_lo[:, t % 2, :, :], rqk[:, t % 2, :, :], rqk_hi[:, t % 2, :, :],
                                              ALU.subtract).then_inc(r_qk_ready, 1)
                        if 2 <= t and c == norm_step(t):
                            hd = t - 2
                            dve.wait_ge(r_ro_done, hd + 1)
                            for f in range(4 * hd, 4 * hd + (4 if t <= RT_HEADS else 1)):
                                normed(f)
                        if t > RT_HEADS and 2 <= c <= 4:
                            normed(4 * (t - 2) + c - 1)
                        if not 1 <= t <= RT_HEADS:
                            continue
                        hd = t - 1
                        if c == 1:
                            dve.wait_ge(r_s_full, hd + 1)
                            dve.wait_ge(r_dec, hd + 1)
                            dve.tensor_tensor(rat[:, :], bank[6][:, 0:384], rdec[:, :], ALU.mult).then_inc(r_at_done, 1)
                            for i in range(2):
                                dve.wait_ge(r_v_hi, 2 * hd + i + 1)
                                dve.tensor_tensor(rv_lo[:, i, :], bank[2 + i][:, :], rv_hi[:, i, :],
                                                  ALU.subtract).then_inc(r_v_ready, 1)
                        if c == 2:
                            dve.wait_ge(r_at_hi, hd + 1)
                            dve.tensor_tensor(rat_lo[:, :], rat[:, :], rat_hi[:, :], ALU.subtract).then_inc(r_at_ready, 1)
                        if c == 5:
                            dve.wait_ge(r_av_full, hd + 1)
                            for i in range(2):
                                at = 4 * hd + 2 * i
                                dve.tensor_copy(ro[:, at:at + 2, :].rearrange("p a t -> p (a t)"),
                                                bank[4 + i][:, :]).then_inc(r_o_done, 1)
                gated(15)
                gated_lo(15)
                out_proj(y, P + 48, 2, 1.0, SEQ)

            layer = 0
            for y, kind in enumerate(PHASES):
                if kind == "ffn":
                    ffn(y)
                elif kind == "mix":
                    mix(y, layer)
                    layer += 1
                elif kind == "final":
                    dve.tensor_tensor(lam_p[:, :, :], lam_in[:, 0:4:2, :], lam_in[:, 1:4:2, :], ALU.mult)\
                       .then_inc(lam_step, 1)
                    dve.wait_ge(lam_step, 1)
                    dve.tensor_reduce(lam2[:, 0:2], lam_p[:, :, :], AX.X, ALU.add).then_inc(lam_step, 1)
                    dve.tensor_scalar(sub_gain, sub_raw, 1.0 - LAM_INIT, None, ALU.mult).then_inc(lam_step, 1)
                    dve.tensor_scalar(q_gain, q_raw, 64 ** -0.5, None, ALU.mult).then_inc(lam_step, 1)
                    dve.wait_ge(R_ready, y + 1)
                    for f in range(KD):
                        dve.scalar_tensor_tensor(out=h[:, f, META:T], in0=h[:, f, META:T], scalar=gain[:, y, f:f + 1],
                                                 in1=R[:, META:T], op0=ALU.mult, op1=ALU.mult).then_inc(h_done, 1)
                    dve.wait_ge(lam_exp, 1)
                    dve.scalar_tensor_tensor(out=lam2[:, 2:3], in0=lam2[:, 1:2], scalar=LAM_INIT, in1=lam2[:, 0:1],
                                             op0=ALU.subtract, op1=ALU.subtract).then_inc(lam_step, 1)
                elif kind == "da":
                    da(y)
                else:
                    rt(y)


        @block.gpsimd
        def _(pool):
            pool_update(pool, 0)
            pool.dma_start(consts[:, 1:7, :], cst[:, 128:7 * 128].rearrange("p (a c) -> p a c", c=128))\
                .then_inc(const_loaded, 16)
            pool.dma_start(sgain[:, :], small[:, GAINS:GAINS + SMALLS]).then_inc(const_loaded, 16)
            pool.dma_start(lam_in[:, :, :], lam.partition_broadcast(128)).then_inc(const_loaded, 16)
            layer = 0
            tables = 0
            for y, kind in enumerate(PHASES):
                if kind in ("mix", "da", "rt"):
                    pool.wait_ge(panel_used, BASE[y]["P"])
                    at = {"mix": 7 * 128, "da": 7 * 128 + SW, "rt": 7 * 128 + SW + 384}[kind]
                    dst = {"mix": smask, "da": dist, "rt": rdist}[kind]
                    w = SW if kind == "mix" else 384
                    pool.dma_start(dst[:, :], cst[:, at:at + w]).then_inc(table_loaded, 16)
                    tables += 1
                if kind == "mix":
                    l, H, W2 = layer, SB_HEADS * layer, win(y + 1)
                    layer += 1
                    pool.memset(cpad[:, :, 0:CPAD], 0.0).then_inc(pad_done, 1)
                    state = {"tap": 0}

                    def taps(count):
                        total, first = len(POOL_CONV) * CONV_K, len(POOL_CONV)
                        for i in range(state["tap"], min(state["tap"] + count, total)):
                            c, k = pool_tap(i)
                            acc = proj[:, A_SLOT + c, W2]
                            if k == 0:
                                pool.wait_ge(cin_done, CH * l + c + 1)
                                pool.tensor_scalar(acc, cpad[:, c, T - width(y + 1):T], conv_w(l, c, 0),
                                                   conv_w(l, c, CONV_K), ALU.mult, ALU.add).then_inc(pool_tap_done, 1)
                            else:
                                pool.wait_ge(tap_product, (total - first) * l + i - first + 1)
                                pool.wait_ge(pool_tap_done, total * l + i - first + 1)
                                pool.tensor_tensor(acc, acc, tprod[:, (i - first) % TAP_RING, W2], ALU.add)\
                                    .then_inc(pool_tap_done, 1)
                            state["tap"] = i + 1

                    taps(len(POOL_CONV) + POOL_TAPS * 11)
                    pool.wait_ge(table_loaded, 16 * tables)
                    for t in range(SB_HEADS + 1):
                        if t < SB_HEADS:
                            pool.wait_ge(nlk_done, H + t + 1)
                            pool.tensor_tensor(nlk[:, :], nlk[:, :], smask[:, :], ALU.mult).then_inc(nlk_masked, 1)
                            taps(POOL_HEAD_TAPS)
                        if t >= 1:
                            pool.wait_ge(ex_done, H + t)
                            pool.tensor_tensor(ex[:, :], ex[:, :], smask[:, :], ALU.mult).then_inc(ex_masked, 1)
                            taps(POOL_HEAD_TAPS)
                        if t == SB_HEADS - 1:
                            assert state["tap"] == len(POOL_CONV) * CONV_K
                            pool.wait_ge(pool_tap_done, len(POOL_CONV) * CONV_K * (l + 1))
                            pool.wait_ge(tap_done, len(DVE_CONV) * CONV_K * (l + 1))
                            for c in range(1, CH):
                                if c > 1:
                                    pool.wait_ge(ysum_step, 3 * l + c - 1)
                                pool.tensor_tensor(sq[:, W2], sq[:, W2] if c > 1 else proj[:, A_SLOT, W2],
                                                   proj[:, A_SLOT + c, W2], ALU.add).then_inc(ysum_step, 1)
                if y + 1 < len(PHASES):
                    pool_update(pool, y + 1)


GAINS = len(PHASES) * KD
SMALLS = 2 * CH * (CONV_K + 3) + 3 + 16
CONST_LOADS = 3


def tables():
    p = np.arange(128)[:, None]
    c = np.arange(128)[None, :]
    one = np.ones((128, 128))
    parts = [one / D, one / 512, one / 128, (p // 64 == c // 64) / 64.0, p == c, one, p > c]
    parts += [(np.arange(w)[None, :] - p > 0) for _, _, w in S_TILES]
    far = 1e30
    for d in (p - c, 128 + p - np.arange(256)[None, :],
              np.arange(256)[None, :] - p, c - p):
        parts.append(np.where(d >= 0, d, far))
    return np.ascontiguousarray(np.concatenate([np.asarray(x, np.float64) for x in parts], 1), np.float32)


def kernel(**inputs):
    import numpy as _np
    import concourse.bacc as _bacc
    from concourse import mybir as _mybir
    from concourse.bass_utils import run_bass_kernel_spmd as _run

    x = {k: _np.asarray(v) for k, v in inputs.items()}

    def panels(w, tiles):
        K, F = w.shape
        parts = K // 128 // tiles
        return w.reshape(parts, tiles, 128, F // 128, 128).transpose(3, 0, 2, 1, 4)            .reshape(F // 128 * parts, 128, tiles * 128)

    def pairs(w):
        q = panels(w, 4)
        return q.reshape(q.shape[0] // 2, 2, 128, 512).transpose(0, 2, 1, 3).reshape(-1, 128, 1024)

    p8, p11 = [], []

    def feed_forward(gate, up, down):
        p8.append(_np.stack([panels(gate, 8), panels(up, 8)], 1).reshape(-1, 128, K8))
        p11.append(panels(down, HALF))

    for l in range(2):
        feed_forward(x["ffn1_w_gate"][l], x["ffn1_w_up"][l], x["ffn1_w_down"][l])
        w = panels(x["w_in"][l], 8)
        p8.append(w[[*range(12, 20), *range(0, 12), *range(28, 36), *range(20, 28)]])
        p8.extend([pairs(x["w_conv_out"][l]), pairs(x["w_attn_out"][l]), panels(x["w_out"][l], 8)])
        feed_forward(x["ffn2_w_gate"][l], x["ffn2_w_up"][l], x["ffn2_w_down"][l])
    for l in range(2):
        w = x["ffn1_w_in_2"][l]
        feed_forward(w[:, :FF], w[:, FF:], x["ffn1_w_out_2"][l])
        if l == 0:
            w = panels(x["da_w_in_2"][0], 8)
            p8.append(w.reshape(3, DA_HEADS, 128, K8).transpose(1, 0, 2, 3).reshape(24, 128, K8))
            p8.append(panels(x["da_w_out_2"][0], 8))
        else:
            w = panels(x["rt_w_in_2"][0], 8)
            order = [t for h in range(RT_HEADS) for t in (2 * h, 2 * h + 1, 8 + 2 * h, 9 + 2 * h, *range(16 + 4 * h, 20 + 4 * h))]
            p8.append(w[order + list(range(32, 48))])
            p8.append(panels(x["rt_w_out_2"][0], 8))
        w = x["ffn2_w_in_2"][l]
        feed_forward(w[:, :FF], w[:, FF:], x["ffn2_w_out_2"][l])

    def column(v):
        return v.reshape(-1, 128).T

    small = [column(x[n][l]) for l in range(2) for n in ("ffn1_norm", "mix_norm", "ffn2_norm")]
    small.append(column(x["final_norm"]))
    small += [column(x[n][l]) for l in range(2) for n in ("ffn1_norm_2", "mix_norm_2", "ffn2_norm_2")]
    for l in range(2):
        per = [column(x["conv_w"][l][k]) for k in range(CONV_K)]
        per += [column(x[n][l]) for n in ("conv_b", "conv_ln_g", "conv_ln_b")]
        small.append(_np.stack(per, 2).reshape(128, -1))
    small += [_np.tile(x["da_q_gain_2"][0], 2)[:, None], _np.tile(x["da_k_gain_2"][0], 2)[:, None],
              x["da_subln_2"][0][:, None], column(x["rt_subln_2"][0])]
    arrays = {
        "w8": _np.concatenate(p8),
        "w11": _np.concatenate(p11),
        "xT": _np.ascontiguousarray(_np.concatenate([x["meta"], x["x"][0]]).T),
        "small": _np.ascontiguousarray(_np.concatenate(small, 1)),
        "cst": tables(),
        "lam": _np.ascontiguousarray(x["da_lambda_2"][0]),
    }
    nc = _bacc.Bacc("TRN2", target_bir_lowering=False, num_devices=1)
    args = [nc.dram_tensor(n, a.shape, _mybir.dt.from_np(a.dtype), kind="ExternalInput").ap() for n, a in arrays.items()]
    out = nc.dram_tensor("outT", (D, SEQ), _mybir.dt.float32, kind="ExternalOutput").ap()
    build(nc, *args, out)
    r = _run(nc, [arrays], core_ids=[0])
    return _np.ascontiguousarray(_np.asarray(r.results[0]["outT"]).T)[None]
```
